# Optimizing a Trainium2 kernel written in Bass

```python
import math
import jax, jax.numpy as jnp
from jax import lax
import numpy as np
import jax
import jax.numpy as jnp

D_MODEL = 1024
BATCH = 1
SEQ = 256
DEPTH = 1

ATTN_HEADS = 6
ATTN_HEAD_DIM = 64
ATTN_WIDTH = ATTN_HEADS * ATTN_HEAD_DIM
MOBA_BLOCK = 256
MOBA_TOPK = 3
MOBA_QUERY_CHUNK = 64
SSD_HEADS = 6
SSD_HEAD_DIM = 64
SSD_WIDTH = SSD_HEADS * SSD_HEAD_DIM
SSD_GROUPS = 2
SSD_STATE = 128
SSD_CONV = 4
SSD_CHUNK = 128
XBC_WIDTH = SSD_WIDTH + 2 * SSD_GROUPS * SSD_STATE
POOL_WINDOWS = (2, 4, 8, 16)
POOL_GROUPS = len(POOL_WINDOWS)
POOL_GROUP_DIM = 64
POOL_WIDTH = POOL_GROUPS * POOL_GROUP_DIM
MIX_WIDTH = ATTN_WIDTH + SSD_WIDTH + POOL_WIDTH
IN_PROJ_WIDTH = 3 * ATTN_WIDTH + SSD_WIDTH + XBC_WIDTH + SSD_HEADS + POOL_WIDTH
FFN_HIDDEN = ((8 * D_MODEL // 3 + 255) // 256) * 256
NORM_EPS = 1e-6
NEG_INF = -1e30


def rmsnorm(x, g):
    xf = x.astype(jnp.float32)
    xf = xf * lax.rsqrt(jnp.mean(xf * xf, axis=-1, keepdims=True) + NORM_EPS)
    return xf.astype(x.dtype) * g

def causal_depthwise_conv(x, w, b):
    k_width, ch = w.shape
    y = lax.conv_general_dilated(
        x, w[:, None, :], window_strides=(1,), padding=[(k_width - 1, 0)],
        dimension_numbers=('NWC', 'WIO', 'NWC'), feature_group_count=ch)
    return y + b

def moba_attention(q, k, v):
    bsz, n_heads, seq, hd = q.shape
    n_blocks = -(-seq // MOBA_BLOCK)
    pad = n_blocks * MOBA_BLOCK - seq
    k_p = jnp.pad(k, ((0, 0), (0, 0), (0, pad), (0, 0)))
    v_p = jnp.pad(v, ((0, 0), (0, 0), (0, pad), (0, 0)))
    k_blocks = k_p.reshape(bsz, n_heads, n_blocks, MOBA_BLOCK, hd)
    v_blocks = v_p.reshape(bsz, n_heads, n_blocks, MOBA_BLOCK, hd)
    k_mean = jnp.mean(k_blocks, axis=3)
    n_sel = min(MOBA_TOPK, n_blocks)
    scale = hd ** -0.5
    b_idx = jnp.arange(bsz)[:, None, None, None]
    h_idx = jnp.arange(n_heads)[None, :, None, None]
    block_ids = jnp.arange(n_blocks)

    def query_chunk(c):
        q0 = c * MOBA_QUERY_CHUNK
        qc = lax.dynamic_slice_in_dim(q, q0, MOBA_QUERY_CHUNK, axis=2)
        blk = q0 // MOBA_BLOCK
        gate = jnp.einsum('bhqd,bhnd->bhqn', qc, k_mean).astype(jnp.float32)
        gate = jnp.where(block_ids < blk, gate, NEG_INF)
        _, idx = lax.top_k(gate, n_sel)
        valid = jnp.arange(n_sel) < blk
        k_sel = k_blocks[b_idx, h_idx, idx]
        v_sel = v_blocks[b_idx, h_idx, idx]
        s_sel = jnp.einsum('bhqd,bhqnkd->bhqnk', qc, k_sel).astype(jnp.float32) * scale
        s_sel = jnp.where(valid[:, None], s_sel, NEG_INF)
        s_sel = s_sel.reshape(bsz, n_heads, MOBA_QUERY_CHUNK, n_sel * MOBA_BLOCK)
        k_own = lax.dynamic_index_in_dim(k_blocks, blk, axis=2, keepdims=False)
        v_own = lax.dynamic_index_in_dim(v_blocks, blk, axis=2, keepdims=False)
        s_own = jnp.einsum('bhqd,bhkd->bhqk', qc, k_own).astype(jnp.float32) * scale
        q_pos = q0 + jnp.arange(MOBA_QUERY_CHUNK)
        k_pos = blk * MOBA_BLOCK + jnp.arange(MOBA_BLOCK)
        s_own = jnp.where(k_pos[None, :] <= q_pos[:, None], s_own, NEG_INF)
        p = jax.nn.softmax(jnp.concatenate([s_sel, s_own], axis=-1), axis=-1).astype(v.dtype)
        p_sel = p[..., :n_sel * MOBA_BLOCK].reshape(bsz, n_heads, MOBA_QUERY_CHUNK, n_sel, MOBA_BLOCK)
        p_own = p[..., n_sel * MOBA_BLOCK:]
        return (jnp.einsum('bhqnk,bhqnkd->bhqd', p_sel, v_sel)
                + jnp.einsum('bhqk,bhkd->bhqd', p_own, v_own))

    out = lax.map(query_chunk, jnp.arange(seq // MOBA_QUERY_CHUNK))
    return out.transpose(1, 0, 3, 2, 4).reshape(bsz, seq, n_heads * hd)

def ssd_mixer(xbc, z, dt_raw, conv_w, conv_b, dt_bias, a_log, d_skip, norm_w):
    bsz, seq, _ = xbc.shape
    n_chunks = seq // SSD_CHUNK
    rep = SSD_HEADS // SSD_GROUPS
    xbc = jax.nn.silu(causal_depthwise_conv(xbc, conv_w, conv_b)).astype(jnp.float32)
    xs, b_in, c_in = jnp.split(xbc, [SSD_WIDTH, SSD_WIDTH + SSD_GROUPS * SSD_STATE], axis=-1)
    x_h = xs.reshape(bsz, seq, SSD_HEADS, SSD_HEAD_DIM)
    b_h = jnp.repeat(b_in.reshape(bsz, seq, SSD_GROUPS, SSD_STATE), rep, axis=2)
    c_h = jnp.repeat(c_in.reshape(bsz, seq, SSD_GROUPS, SSD_STATE), rep, axis=2)
    dt = jax.nn.softplus(dt_raw.astype(jnp.float32) + dt_bias.astype(jnp.float32))
    a = -jnp.exp(a_log.astype(jnp.float32))

    def chunks(t):
        return t.reshape((bsz, n_chunks, SSD_CHUNK) + t.shape[2:])

    xdt = chunks(x_h * dt[..., None])
    b_c, c_c = chunks(b_h), chunks(c_h)
    a_cum = jnp.cumsum(chunks(dt * a).transpose(0, 3, 1, 2), axis=-1)
    causal = jnp.tril(jnp.ones((SSD_CHUNK, SSD_CHUNK), dtype=bool))
    decay = jnp.exp(jnp.where(causal, a_cum[..., :, None] - a_cum[..., None, :], -jnp.inf))
    y_diag = jnp.einsum('bclhn,bcshn,bhcls,bcshp->bclhp', c_c, b_c, decay, xdt)
    decay_to_end = jnp.exp(a_cum[..., -1:] - a_cum)
    states = jnp.einsum('bclhn,bhcl,bclhp->bchpn', b_c, decay_to_end, xdt)
    chunk_decay = jnp.exp(a_cum[..., -1])

    def step(h, inp):
        st, d = inp
        return h * d[..., None, None] + st, h

    _, prev = lax.scan(step, jnp.zeros_like(states[:, 0]),
                       (states.transpose(1, 0, 2, 3, 4), chunk_decay.transpose(2, 0, 1)))
    prev = prev.transpose(1, 0, 2, 3, 4)
    y_off = jnp.einsum('bclhn,bchpn,bhcl->bclhp', c_c, prev, jnp.exp(a_cum))
    y = (y_diag + y_off).reshape(bsz, seq, SSD_HEADS, SSD_HEAD_DIM) + x_h * d_skip.astype(jnp.float32)[:, None]
    y = y.reshape(bsz, seq, SSD_WIDTH) * jax.nn.silu(z.astype(jnp.float32))
    yg = y.reshape(bsz, seq, SSD_GROUPS, SSD_WIDTH // SSD_GROUPS)
    yg = yg * lax.rsqrt(jnp.mean(yg * yg, axis=-1, keepdims=True) + NORM_EPS)
    return (yg.reshape(bsz, seq, SSD_WIDTH) * norm_w.astype(jnp.float32)).astype(z.dtype)

def pool_mixer(p, pool_w, pool_scale):
    bsz, seq, _ = p.shape
    pg = p.astype(jnp.float32).reshape(bsz, seq, POOL_GROUPS, POOL_GROUP_DIM)
    csum = jnp.concatenate([jnp.zeros_like(pg[:, :1]), jnp.cumsum(pg, axis=1)], axis=1)
    t = jnp.arange(seq)[:, None]
    win = jnp.asarray(POOL_WINDOWS, dtype=jnp.int32)[None, :]
    start = jnp.maximum(t + 1 - win, 0)
    lower = csum[:, start, jnp.arange(POOL_GROUPS)[None, :], :]
    count = jnp.minimum(t + 1, win).astype(jnp.float32)
    mean = (csum[:, 1:] - lower) / count[None, :, :, None]
    mixed = jnp.einsum('bsgc,gcd->bsgd', mean - pg, pool_w.astype(jnp.float32))
    return (mixed.reshape(bsz, seq, POOL_WIDTH) * pool_scale.astype(jnp.float32)).astype(p.dtype)

def hybrid_layer(x, norm_mix, w_in, conv_w, conv_b, dt_bias, a_log, d_skip, ssd_norm,
                 pool_w, pool_scale, w_out, norm_ffn, w_gate_up, w_down):
    bsz, seq, _ = x.shape
    h = rmsnorm(x, norm_mix)
    u = h @ w_in
    sizes = (ATTN_WIDTH, ATTN_WIDTH, ATTN_WIDTH, SSD_WIDTH, XBC_WIDTH, SSD_HEADS, POOL_WIDTH)
    offsets = []
    acc = 0
    for s in sizes[:-1]:
        acc += s
        offsets.append(acc)
    q, k, v, z, xbc, dt_raw, p_in = jnp.split(u, offsets, axis=-1)

    def heads(t):
        return t.reshape(bsz, seq, ATTN_HEADS, ATTN_HEAD_DIM).transpose(0, 2, 1, 3)

    y_attn = moba_attention(heads(q), heads(k), heads(v))
    y_ssd = ssd_mixer(xbc, z, dt_raw, conv_w, conv_b, dt_bias, a_log, d_skip, ssd_norm)
    y_pool = pool_mixer(p_in, pool_w, pool_scale)
    x = x + jnp.concatenate([y_attn, y_ssd, y_pool], axis=-1) @ w_out
    h = rmsnorm(x, norm_ffn)
    gate, up = jnp.split(h @ w_gate_up, 2, axis=-1)
    return x + (jax.nn.silu(gate) * up) @ w_down

def first_inputs(seed: int = 0) -> dict:
    key = jax.random.key(seed)
    ks = jax.random.split(key, 16)
    nrm = jax.random.normal
    dt0 = jnp.exp(jax.random.uniform(ks[5], (DEPTH, SSD_HEADS), minval=math.log(1e-3), maxval=math.log(1e-1)))
    return {
        'x': nrm(ks[0], (BATCH, SEQ, D_MODEL), jnp.float32),
        'norm_mix': 1.0 + 0.05 * nrm(ks[1], (DEPTH, D_MODEL), jnp.float32),
        'w_in': nrm(ks[2], (DEPTH, D_MODEL, IN_PROJ_WIDTH), jnp.float32) * D_MODEL ** -0.5,
        'conv_w': nrm(ks[3], (DEPTH, SSD_CONV, XBC_WIDTH), jnp.float32) * SSD_CONV ** -0.5,
        'conv_b': 0.02 * nrm(ks[4], (DEPTH, XBC_WIDTH), jnp.float32),
        'dt_bias': dt0 + jnp.log(-jnp.expm1(-dt0)),
        'a_log': jnp.log(jax.random.uniform(ks[6], (DEPTH, SSD_HEADS), minval=1.0, maxval=16.0)),
        'd_skip': 1.0 + 0.1 * nrm(ks[7], (DEPTH, SSD_HEADS), jnp.float32),
        'ssd_norm': 1.0 + 0.05 * nrm(ks[8], (DEPTH, SSD_WIDTH), jnp.float32),
        'pool_w': nrm(ks[9], (DEPTH, POOL_GROUPS, POOL_GROUP_DIM, POOL_GROUP_DIM), jnp.float32) * POOL_GROUP_DIM ** -0.5,
        'pool_scale': 1.0 + 0.1 * nrm(ks[10], (DEPTH, POOL_WIDTH), jnp.float32),
        'w_out': nrm(ks[11], (DEPTH, MIX_WIDTH, D_MODEL), jnp.float32) * MIX_WIDTH ** -0.5,
        'norm_ffn': 1.0 + 0.05 * nrm(ks[12], (DEPTH, D_MODEL), jnp.float32),
        'w_gate_up': nrm(ks[13], (DEPTH, D_MODEL, 2 * FFN_HIDDEN), jnp.float32) * D_MODEL ** -0.5,
        'w_down': nrm(ks[14], (DEPTH, FFN_HIDDEN, D_MODEL), jnp.float32) * FFN_HIDDEN ** -0.5,
        'norm_final': 1.0 + 0.05 * nrm(ks[15], (D_MODEL,), jnp.float32),
    }

def first_block(x, norm_mix, w_in, conv_w, conv_b, dt_bias, a_log, d_skip, ssd_norm,
              pool_w, pool_scale, w_out, norm_ffn, w_gate_up, w_down, norm_final):
    for l in range(DEPTH):
        x = hybrid_layer(x, norm_mix[l], w_in[l], conv_w[l], conv_b[l], dt_bias[l], a_log[l],
                         d_skip[l], ssd_norm[l], pool_w[l], pool_scale[l], w_out[l],
                         norm_ffn[l], w_gate_up[l], w_down[l])
    return rmsnorm(x, norm_final)


CTX_LEN = 256
GRID_W = 64
N_HEADS = 8
HEAD_DIM = 64
D_ATTN = N_HEADS * 2 * HEAD_DIM
D_HYENA = D_MODEL
SHORT_CONV = 3
FILTER_EMB = 33
FILTER_ORDER = 64
DECAY_TARGET = 1e-2
FAST_DECAY_PCT = 0.3
SLOW_DECAY_PCT = 1.5
D_FF = 2816
ROPE_THETA = 10000.0
Q_BLOCK = 128
N_MOD = 9
N_PROJ = 3 * D_HYENA + 3 * D_ATTN + 2 * D_MODEL
SPLITS = (3 * D_HYENA, 3 * D_HYENA + D_ATTN, 3 * D_HYENA + 2 * D_ATTN, 3 * D_HYENA + 3 * D_ATTN)
EPS = 1e-6


def rmsnorm_2(x, g):
    xf = x.astype(jnp.float32)
    y = xf * lax.rsqrt(jnp.mean(xf * xf, axis=-1, keepdims=True) + EPS)
    return (y * g.astype(jnp.float32)).astype(x.dtype)

def modulate(x, shift, scale):
    return x * (1.0 + scale) + shift

def swiglu(x, w_in, w_out):
    gate, up = jnp.split(x @ w_in, 2, axis=-1)
    return (jax.nn.silu(gate) * up) @ w_out

def ffn_half(s, shift, scale, gate, g_pre, g_post, w_in, w_out):
    h = swiglu(modulate(rmsnorm_2(s, g_pre), shift, scale), w_in, w_out)
    return s + 0.5 * gate * rmsnorm_2(h, g_post)

def short_conv(x, w, b):
    L = x.shape[1]
    pad = SHORT_CONV // 2
    xp = jnp.pad(x, ((0, 0), (pad, pad), (0, 0)))
    return sum(xp[:, j:j + L] * w[j] for j in range(SHORT_CONV)) + b

def hyena_kernel(L, w1, b1, w2, b2, w3, b3, w4, freq):
    f32 = jnp.float32
    bands = (FILTER_EMB - 1) // 2
    t = jnp.linspace(0.0, 1.0, L, dtype=f32)[:, None]
    w = 2.0 * math.pi * jnp.arange(L, dtype=f32)[:, None] / L
    f = jnp.linspace(1e-4, bands - 1, bands, dtype=f32)[None, :]
    z = jnp.concatenate([t, jnp.cos(f * w), -jnp.sin(f * w)], axis=-1)
    h = jnp.sin(freq * (z @ w1 + b1))
    h = jnp.sin(freq * (h @ w2 + b2))
    h = jnp.sin(freq * (h @ w3 + b3))
    h = (h @ w4).astype(f32)
    deltas = jnp.linspace(math.log(DECAY_TARGET) / SLOW_DECAY_PCT,
                          math.log(DECAY_TARGET) / FAST_DECAY_PCT, D_HYENA, dtype=f32)
    decay = jnp.exp(-t * jnp.abs(deltas))
    h_fwd, h_bwd = jnp.split(h, 2, axis=-1)
    h_fwd = h_fwd * decay
    h_bwd = h_bwd * decay
    k = jnp.concatenate([h_fwd, jnp.zeros_like(h_fwd[:1]), h_bwd[:0:-1]], axis=0)
    return k / (jnp.sum(jnp.abs(k), axis=0, keepdims=True) + EPS)

def bidir_long_conv(u, k):
    L = u.shape[1]
    uf = jnp.fft.rfft(u.astype(jnp.float32), n=2 * L, axis=1)
    kf = jnp.fft.rfft(k, n=2 * L, axis=0)
    y = jnp.fft.irfft(uf * kf[None], n=2 * L, axis=1)[:, :L]
    return y.astype(u.dtype)

def hyena_branch(z_hy, conv_w, conv_b, filt, hy_bias):
    z = short_conv(z_hy, conv_w, conv_b)
    x0, x1, v = jnp.split(z, 3, axis=-1)
    k = hyena_kernel(z.shape[1], *filt)
    u = v * x1
    y = bidir_long_conv(u, k) + u * hy_bias
    return y * x0

def axial_rope_tables(L):
    rows = L // GRID_W
    r, col = jnp.meshgrid(jnp.arange(rows), jnp.arange(GRID_W), indexing='ij')
    r = r.reshape(-1).astype(jnp.float32)
    col = col.reshape(-1).astype(jnp.float32)
    half = HEAD_DIM // 2
    inv = ROPE_THETA ** (-jnp.arange(0, half, 2, dtype=jnp.float32) / half)
    ang = jnp.stack([r[:, None] * inv, col[:, None] * inv], axis=1)
    return jnp.cos(ang), jnp.sin(ang)

def apply_axial_rope(x, cos, sin):
    B, L = x.shape[:2]
    xr = x.reshape(B, L, N_HEADS, 2, 2, 2, HEAD_DIM // 4)
    x0, x1 = xr[..., 0, :], xr[..., 1, :]
    c = cos[None, :, None, None]
    s = sin[None, :, None, None]
    out = jnp.stack([x0 * c - x1 * s, x0 * s + x1 * c], axis=-2)
    return out.reshape(x.shape).astype(x.dtype)

def diff_attention(q, k, v, lam):
    B, L = q.shape[:2]
    nb = L // Q_BLOCK
    qb = jnp.moveaxis(q.reshape(B, nb, Q_BLOCK, N_HEADS, 2, HEAD_DIM), 1, 0)

    def block(qblk):
        s = jnp.einsum('bqhmd,bkhmd->bhmqk', qblk, k).astype(jnp.float32) * (HEAD_DIM ** -0.5)
        p = jax.nn.softmax(s, axis=-1)
        p = p[:, :, 0] - lam * p[:, :, 1]
        return jnp.einsum('bhqk,bkhe->bqhe', p.astype(v.dtype), v)

    o = lax.map(block, qb)
    return jnp.moveaxis(o, 0, 1).reshape(B, L, N_HEADS, 2 * HEAD_DIM)

def context_kv(h, w_in):
    B, L = h.shape[:2]
    k, v = jnp.split(h @ w_in[:, SPLITS[1]:SPLITS[3]], 2, axis=-1)
    return k.reshape(B, L, N_HEADS, 2, HEAD_DIM), v.reshape(B, L, N_HEADS, 2 * HEAD_DIM)

def token_mixer(h, w_in, conv_w, conv_b, filt, hy_bias, lam, lam_init, subln_g,
                w_hy_out, w_da_out, w_o, rope, ctx_kv):
    B, L = h.shape[:2]
    z_hy, q, k, v, gates = jnp.split(h @ w_in, SPLITS, axis=-1)
    y_hy = hyena_branch(z_hy, conv_w, conv_b, filt, hy_bias) @ w_hy_out
    q = q.reshape(B, L, N_HEADS, 2, HEAD_DIM)
    k = k.reshape(B, L, N_HEADS, 2, HEAD_DIM)
    v = v.reshape(B, L, N_HEADS, 2 * HEAD_DIM)
    if rope is not None:
        q = apply_axial_rope(q, *rope)
        k = apply_axial_rope(k, *rope)
    if ctx_kv is not None:
        k = jnp.concatenate([k, ctx_kv[0]], axis=1)
        v = jnp.concatenate([v, ctx_kv[1]], axis=1)
    o = diff_attention(q, k, v, lam)
    o = rmsnorm_2(o, subln_g) * (1.0 - lam_init)
    y_da = o.reshape(B, L, D_ATTN) @ w_da_out
    g_hy, g_da = jnp.split(jax.nn.sigmoid(gates), 2, axis=-1)
    return (g_hy * y_hy + g_da * y_da) @ w_o

def second_inputs(seed: int = 0) -> dict:
    key = jax.random.key(seed)
    ks = jax.random.split(key, 32)
    f32 = jnp.float32

    def nrm(k, shape, scale):
        return jax.random.normal(k, shape, f32) * scale

    return {
        'x': nrm(ks[0], (BATCH, SEQ, D_MODEL), 1.0),
        'c': nrm(ks[1], (BATCH, D_MODEL), 1.0),
        'ctx': nrm(ks[2], (BATCH, CTX_LEN, D_MODEL), 1.0),
        'c_ctx': nrm(ks[3], (D_MODEL,), 1.0),
        'w_ada': nrm(ks[4], (DEPTH, D_MODEL, N_MOD * D_MODEL), 0.5 * D_MODEL ** -0.5),
        'b_ada': nrm(ks[5], (DEPTH, N_MOD * D_MODEL), 0.01),
        'norm_g': 1.0 + nrm(ks[6], (DEPTH, 6, D_MODEL), 0.02),
        'w_ff_in': nrm(ks[7], (DEPTH, 2, D_MODEL, 2 * D_FF), D_MODEL ** -0.5),
        'w_ff_out': nrm(ks[8], (DEPTH, 2, D_FF, D_MODEL), D_FF ** -0.5),
        'w_in': nrm(ks[9], (DEPTH, D_MODEL, N_PROJ), D_MODEL ** -0.5),
        'hy_conv_w': nrm(ks[10], (DEPTH, SHORT_CONV, 3 * D_HYENA), SHORT_CONV ** -0.5),
        'hy_conv_b': nrm(ks[11], (DEPTH, 3 * D_HYENA), 0.01),
        'filt_w1': nrm(ks[12], (DEPTH, FILTER_EMB, FILTER_ORDER), FILTER_EMB ** -0.5),
        'filt_b1': nrm(ks[13], (DEPTH, FILTER_ORDER), 0.1),
        'filt_w2': nrm(ks[14], (DEPTH, FILTER_ORDER, FILTER_ORDER), FILTER_ORDER ** -0.5),
        'filt_b2': nrm(ks[15], (DEPTH, FILTER_ORDER), 0.1),
        'filt_w3': nrm(ks[16], (DEPTH, FILTER_ORDER, FILTER_ORDER), FILTER_ORDER ** -0.5),
        'filt_b3': nrm(ks[17], (DEPTH, FILTER_ORDER), 0.1),
        'filt_w4': nrm(ks[18], (DEPTH, FILTER_ORDER, 2 * D_HYENA), FILTER_ORDER ** -0.5),
        'filt_freq': 1.0 + nrm(ks[19], (DEPTH, FILTER_ORDER), 0.01),
        'hy_bias': nrm(ks[20], (DEPTH, D_HYENA), 0.1),
        'lambda_q1': nrm(ks[21], (DEPTH, HEAD_DIM), 0.1),
        'lambda_k1': nrm(ks[22], (DEPTH, HEAD_DIM), 0.1),
        'lambda_q2': nrm(ks[23], (DEPTH, HEAD_DIM), 0.1),
        'lambda_k2': nrm(ks[24], (DEPTH, HEAD_DIM), 0.1),
        'subln_g': 1.0 + nrm(ks[25], (DEPTH, 2 * HEAD_DIM), 0.02),
        'w_hy_out': nrm(ks[26], (DEPTH, D_HYENA, D_MODEL), D_HYENA ** -0.5),
        'w_da_out': nrm(ks[27], (DEPTH, D_ATTN, D_MODEL), D_ATTN ** -0.5),
        'w_o': nrm(ks[28], (DEPTH, D_MODEL, D_MODEL), D_MODEL ** -0.5),
    }

def second_block(x, c, ctx, c_ctx, w_ada, b_ada, norm_g, w_ff_in, w_ff_out, w_in,
              hy_conv_w, hy_conv_b, filt_w1, filt_b1, filt_w2, filt_b2, filt_w3, filt_b3,
              filt_w4, filt_freq, hy_bias, lambda_q1, lambda_k1, lambda_q2, lambda_k2,
              subln_g, w_hy_out, w_da_out, w_o):
    rope = axial_rope_tables(x.shape[1])
    xs, cs = x, ctx
    for l in range(DEPTH):
        lam_init = 0.8 - 0.6 * math.exp(-0.3 * l)
        lam = (jnp.exp(jnp.sum(lambda_q1[l] * lambda_k1[l]).astype(jnp.float32))
               - jnp.exp(jnp.sum(lambda_q2[l] * lambda_k2[l]).astype(jnp.float32)) + lam_init)
        mod_x = jnp.split((jax.nn.silu(c) @ w_ada[l] + b_ada[l])[:, None, :], N_MOD, axis=-1)
        mod_c = jnp.split((jax.nn.silu(c_ctx) @ w_ada[l] + b_ada[l])[None, None, :], N_MOD, axis=-1)
        g = norm_g[l]
        filt = (filt_w1[l], filt_b1[l], filt_w2[l], filt_b2[l], filt_w3[l], filt_b3[l],
                filt_w4[l], filt_freq[l])
        mixer_params = (w_in[l], hy_conv_w[l], hy_conv_b[l], filt, hy_bias[l], lam, lam_init,
                        subln_g[l], w_hy_out[l], w_da_out[l], w_o[l])
        xs = ffn_half(xs, mod_x[0], mod_x[1], mod_x[2], g[0], g[1], w_ff_in[l, 0], w_ff_out[l, 0])
        cs = ffn_half(cs, mod_c[0], mod_c[1], mod_c[2], g[0], g[1], w_ff_in[l, 0], w_ff_out[l, 0])
        hx = modulate(rmsnorm_2(xs, g[2]), mod_x[3], mod_x[4])
        hc = modulate(rmsnorm_2(cs, g[2]), mod_c[3], mod_c[4])
        y = token_mixer(hx, *mixer_params, rope, context_kv(hc, w_in[l]))
        xs = xs + mod_x[5] * rmsnorm_2(y, g[3])
        if l < DEPTH - 1:
            yc = token_mixer(hc, *mixer_params, None, None)
            cs = cs + mod_c[5] * rmsnorm_2(yc, g[3])
            cs = ffn_half(cs, mod_c[6], mod_c[7], mod_c[8], g[4], g[5], w_ff_in[l, 1], w_ff_out[l, 1])
        xs = ffn_half(xs, mod_x[6], mod_x[7], mod_x[8], g[4], g[5], w_ff_in[l, 1], w_ff_out[l, 1])
    return xs


def setup_inputs(seed=0):
    out = dict(first_inputs(seed))
    for name, value in second_inputs(seed + 1).items():
        if name != "x":
            out[name + "_2"] = value
    return out


def reference(
    x, norm_mix, w_in, conv_w, conv_b, dt_bias, a_log, d_skip, ssd_norm, pool_w, pool_scale,
    w_out, norm_ffn, w_gate_up, w_down, norm_final, c_2, ctx_2, c_ctx_2, w_ada_2, b_ada_2,
    norm_g_2, w_ff_in_2, w_ff_out_2, w_in_2, hy_conv_w_2, hy_conv_b_2, filt_w1_2, filt_b1_2,
    filt_w2_2, filt_b2_2, filt_w3_2, filt_b3_2, filt_w4_2, filt_freq_2, hy_bias_2, lambda_q1_2,
    lambda_k1_2, lambda_q2_2, lambda_k2_2, subln_g_2, w_hy_out_2, w_da_out_2, w_o_2,
):
    x = first_block(
        x, norm_mix, w_in, conv_w, conv_b, dt_bias, a_log, d_skip, ssd_norm, pool_w, pool_scale,
        w_out, norm_ffn, w_gate_up, w_down, norm_final,
    )
    return second_block(
        x, c_2, ctx_2, c_ctx_2, w_ada_2, b_ada_2, norm_g_2, w_ff_in_2, w_ff_out_2, w_in_2,
        hy_conv_w_2, hy_conv_b_2, filt_w1_2, filt_b1_2, filt_w2_2, filt_b2_2, filt_w3_2,
        filt_b3_2, filt_w4_2, filt_freq_2, hy_bias_2, lambda_q1_2, lambda_k1_2, lambda_q2_2,
        lambda_k2_2, subln_g_2, w_hy_out_2, w_da_out_2, w_o_2,
    )


_drawn_inputs = setup_inputs


def setup_inputs(seed=0):
    import zlib

    import numpy as np

    out = dict(_drawn_inputs(seed))
    spreads = {}
    factors = {'conv_b': 3.688,
     'b_ada_2': 3.528,
     'norm_g_2': 4.758,
     'hy_conv_b_2': 8.0,
     'filt_b1_2': 6.502,
     'filt_b2_2': 5.885,
     'filt_b3_2': 4.794,
     'filt_freq_2': 8.0,
     'lambda_k1_2': 8.0,
     'subln_g_2': 8.0}
    for name, (base, spread) in spreads.items():
        noise = np.random.default_rng([zlib.crc32(name.encode()), seed]).standard_normal(out[name].shape)
        drawn = base * np.exp(spread * noise) if base else spread * noise
        out[name] = jnp.asarray(drawn.astype(out[name].dtype))
    for name, factor in factors.items():
        out[name] = (out[name] * factor).astype(out[name].dtype)
    return out
```

```python
from contextlib import ExitStack

import numpy as np

import concourse.bass as bass
from concourse import mybir

F32 = mybir.dt.float32
F32R = mybir.dt.float32r
ALU = mybir.AluOpType
ACT = mybir.ActivationFunctionType
AX = mybir.AxisListType

P = 128
D = 1024
KD = D // P
T = 256
FH = 2816
KH = FH // P
KHH = KH // 2
RAW = 4
HL = 2
BANKS = 4
EPS = 1e-6
NEG = -1e30
HEADS1 = 6
NT1 = 3
HEADS2 = 8
LAM_INIT = 0.2

Q1, K1, V1, Z1, XBC1, POOL1, DT1 = 0, 3, 6, 9, 12, 19, 21
N_IN1 = 22
HEAD_SLABS = 6

_WIDTHS = [("norm_mix", 8), ("norm_ffn", 8), ("norm_final", 8), ("conv_w", 28), ("conv_b", 7),
           ("d_skip", 3), ("ssd_norm", 3), ("pool_scale", 2), ("b_ada", 72), ("norm_g", 48),
           ("hy_w", 72), ("hy_b", 24), ("hy_bias", 8), ("filt_b", 3), ("filt_freq", 1),
           ("subln", 1), ("dt_bias", 1), ("a_log", 1), ("lam_q", 2), ("lam_k", 2),
           ("filt_w1", 64), ("filt_w2", 64), ("filt_w3", 64)]
COL, NPAR = {}, 0
for _n, _w in _WIDTHS:
    COL[_n] = NPAR
    NPAR += _w

CONSTS = [("ones", 128), ("ident", 128), ("tri", 128), ("mask384", 384), ("maskT", 128),
          ("eps", 1), ("one", 1), ("zero", 8)]
CC, NCON = {}, 0
for _n, _w in CONSTS:
    CC[_n] = NCON
    NCON += _w


def constants():
    a = np.arange(P)
    c = np.zeros((P, NCON), np.float32)
    c[:, CC["ones"]:CC["ones"] + 128] = 1.0
    c[:, CC["ident"]:CC["ident"] + 128] = np.eye(P)
    c[:, CC["tri"]:CC["tri"] + 128] = a[:, None] <= a[None, :]
    causal = np.where(a[None, :] <= a[:, None], 0.0, NEG)
    c[:, CC["mask384"]:CC["mask384"] + 128] = causal
    c[:, CC["mask384"] + 256:CC["mask384"] + 384] = causal
    c[:, CC["maskT"]:CC["maskT"] + 128] = causal.T
    c[:, CC["eps"]] = EPS
    c[:, CC["one"]] = 1.0
    t = np.arange(T)
    rcount = np.zeros((P, 2, T), np.float32)
    for g, w in enumerate((2, 4, 8, 16)):
        rcount[64 * (g % 2):64 * (g % 2) + 64, g // 2] = 1.0 / np.minimum(t + 1, w)
    p = np.arange(P)
    axis, half, i = p // 32 % 2, p // 16 % 2, p % 16
    inv = (np.float32(10000.0) ** (-(2 * i).astype(np.float32) / np.float32(32))).astype(np.float32)
    pos = np.where(axis[:, None] == 0, t[None, :] // 64, t[None, :] % 64).astype(np.float32)
    ang = (pos * inv[:, None]).astype(np.float32).astype(np.float64)
    rope = np.zeros((P, 2, T), np.float32)
    rope[:, 0] = np.cos(ang)
    rope[:, 1] = np.where(half[:, None] == 0, -np.sin(ang), np.sin(ang))
    th = np.pi * (2 * t[None, :] + 1) * t[:, None] / 512.0
    dft = np.zeros((P, 8, T), np.float32)
    dft[:, 0:2] = np.cos(th).reshape(2, P, T).transpose(1, 0, 2)
    dft[:, 2:4] = np.sin(th).reshape(2, P, T).transpose(1, 0, 2)
    dft[:, 4:6] = (np.cos(th).T / 256).reshape(2, P, T).transpose(1, 0, 2)
    dft[:, 6:8] = (np.sin(th).T / 256).reshape(2, P, T).transpose(1, 0, 2)
    bands = 16
    tl = np.linspace(0.0, 1.0, T, dtype=np.float32)[:, None]
    w = (2.0 * np.pi * t.astype(np.float32)[:, None] / T).astype(np.float32)
    f = np.linspace(1e-4, bands - 1, bands, dtype=np.float32)[None, :]
    z = np.concatenate([tl, np.cos(f * w), -np.sin(f * w)], axis=-1).astype(np.float32)
    zt = np.zeros((64, T), np.float32)
    zt[:33] = z.T
    deltas = np.linspace(np.log(1e-2) / 1.5, np.log(1e-2) / 0.3, D, dtype=np.float32)
    decay = np.exp(-tl * np.abs(deltas)[None]).astype(np.float32).reshape(2, P, D).transpose(1, 0, 2)
    return dict(consts=c, rcount=rcount, rope=rope, dft=dft, filt_z=zt, decay=np.ascontiguousarray(decay))


IN2 = {"hy_x0": 0, "hy_x1": 8, "hy_v": 16, "q2": 24, "k2": 32, "v2": 40, "gate2": 48}


class Stage:

    def __init__(self, name, slabs, kt=KD, per_out=1, cols=T, body=4, first=None):
        self.name, self.slabs, self.kt, self.per_out = name, slabs, kt, per_out
        self.weights = "in2" if name in IN2 else name.replace("_head", "")
        self.cols, self.body = cols, body
        self.first = IN2.get(name, 0) if first is None else first
        self.trips = slabs // body
        assert self.trips * body == slabs


def plan():
    st = [Stage("in1_head", HEAD_SLABS, body=HEAD_SLABS),
          Stage("in1", N_IN1 - HEAD_SLABS, first=HEAD_SLABS),
          Stage("out1", KD), Stage("up1", 2 * KH), Stage("down1", 2 * KD, kt=KHH, per_out=2),
          Stage("up2", 2 * KH, cols=2 * T), Stage("down2", 2 * KD, kt=KHH, per_out=2, cols=2 * T),
          Stage("hy_x1", 8), Stage("hy_v", 8), Stage("hy_x0", 8),
          Stage("k2", 8, cols=2 * T), Stage("q2", 8), Stage("v2", 8, cols=2 * T), Stage("gate2", 16),
          Stage("da_out", 8), Stage("hy_out", 8), Stage("o2", 8),
          Stage("up3", 2 * KH), Stage("down3", 2 * KD, kt=KHH, per_out=2)]
    s = 0
    uses = [0] * BANKS
    for n, x in enumerate(st):
        x.s0, x.uses0 = s, list(uses)
        x.next = st[n + 1] if n + 1 < len(st) else None
        s += x.slabs
        for k in range(x.body // x.per_out):
            uses[k % BANKS] += x.trips
        x.uses1, x.s1 = list(uses), s
    return {x.name: x for x in st}, st


NORMS = ["mix1", "ffn1", "final1", "pre2x", "pre2c", "post2x", "post2c", "mod2x", "mod2c",
         "post_mix2", "pre3", "post3"]


def build(nc, d, out):
    stages, order = plan()
    with ExitStack() as ctx:
        def keep(name, shape, dt=F32):
            return ctx.enter_context(nc.sbuf_tensor(name, shape, dt))

        def place(at, name, shape, dt=F32):
            with ExitStack() as held:
                if at:
                    held.enter_context(nc.sbuf_tensor(f"below_{name}", [P, at // 4], F32))
                return held.enter_context(nc.sbuf_tensor(name, shape, dt))

        names = {}

        def sem(name):
            if name not in names:
                names[name] = ctx.enter_context(nc.semaphore(name))
            return names[name]

        KB = 1024
        xT = keep("xT", [P, KD, 2 * T])
        con = keep("con", [P, NCON])
        par = keep("par", [P, NPAR])
        mod = keep("mod", [P, 9, KD, 2])
        gmod = keep("gmod", [P, 9, KD])
        small = keep("small", [P, 256])
        act_c = keep("act_c", [P, KD, 2])
        rinv = keep("rinv", [P, T])
        rtmp = keep("rtmp", [P, T])
        raw = keep("raw", [P, RAW, KHH * P])
        hi = keep("hi", [P, HL, KHH * P], F32R)
        lo = keep("lo", [P, HL, KHH * P], F32R)
        nl = keep("nl", [P, KD, 2 * T], F32R)
        proj = place(0, "proj", [P, KD, 2 * T])
        decay = place(0, "decay_s", [P, 2, D])
        w4 = place(8 * KB, "w4_s", [64, 2 * D])
        nh = keep("nh", [P, KD, 2 * T], F32R)

        sq = place(0, "sq", [P, KD, T])
        xg = place(8 * KB, "xg", [P, KD, T])
        u1 = place(0, "u1", [P, N_IN1, T])
        cT = place(22 * KB, "cT", [P, 7, T])
        mixT = place(29 * KB, "mixT", [P, KD, T])
        vtok = place(37 * KB, "vtok", [P, 2, 384])
        scor = place(40 * KB, "scor", [P, 2, 384])
        prob = place(43 * KB, "prob", [P, 2, 384])
        pT = place(46 * KB, "pT", [P, 2, 384])
        rcount = place(49 * KB, "rcount_s", [P, 2, T])
        poolw = place(51 * KB, "poolw", [P, 2, P])
        seg = place(52 * KB, "seg", [P, 12, P])
        triA = place(58 * KB, "triA", [P, 12, P])
        CE = place(64 * KB, "CE", [P, 6, P])
        xdt = place(67 * KB, "xdt", [P, 2, 384])
        xw = place(70 * KB, "xw", [P, 384])
        prev = place(71 * KB + 512, "prev", [P, 384])
        btok = place(73 * KB, "btok", [P, 2, P])
        dtA = place(74 * KB, "dtA", [8, 4, T])
        pools = place(78 * KB, "pools", [P, 6, T])
        yssd = place(84 * KB, "yssd", [P, 3, T])
        ysq = place(87 * KB, "ysq", [P, 3, T])
        yroot = place(58 * KB, "yroot", [P, 2, T])
        yrg = place(60 * KB, "yrg", [P, 2, T])
        ada = place(90 * KB, "ada", [P, 4, KD * P])
        hh1 = place(0, "hh1", [P, KH, T], F32R)
        hl1 = place(22 * KB, "hl1", [P, KH, T], F32R)
        sg1 = place(44 * KB, "sg1", [P, 2, T])
        pr1 = place(46 * KB, "pr1", [P, 2, T])
        hh2 = place(0, "hh2", [P, KH, 2 * T], F32R)
        hl2 = place(44 * KB, "hl2", [P, KH, 2 * T], F32R)
        sg2 = place(88 * KB, "sg2", [P, 2, 2 * T])
        pr2 = place(92 * KB, "pr2", [P, 2, 2 * T])
        u = place(0, "u", [P, KD, T])
        x0 = place(8 * KB, "x0", [P, KD, T])
        gT = place(16 * KB, "gT", [P, 2 * KD, T])
        rope = place(32 * KB, "rope_s", [P, 2, T])
        dft = place(34 * KB, "dft_s", [P, 8, T])
        otok = place(42 * KB, "otok", [P, 2 * HEADS2, P])
        qT = place(50 * KB, "qT", [P, KD, T])
        kT = place(58 * KB, "kT", [P, KD, 2 * T])
        V = place(74 * KB, "V", [P, 4, D])
        cvt = place(90 * KB, "cvt", [P, 4, T])
        rot = place(94 * KB, "rot", [P, 2, 2, T])
        p2 = place(90 * KB, "p2", [P, 2, 2, 2 * T])
        pT2 = place(98 * KB, "pT2", [P, 2, 4, P])
        kre = place(50 * KB, "kre", [P, 2, D])
        kim = place(58 * KB, "kim", [P, 2, D])
        absk = place(50 * KB, "absk", [P, 2, 2 * D])
        hfb = place(66 * KB, "hfb", [P, 2, 2 * D])
        hsd = place(82 * KB, "hsd", [P, 2, 2 * D])
        filt = place(98 * KB, "filt", [64, 5, T])
        zT = place(104 * KB, "zT", [64, T])
        utok = place(66 * KB, "utok", [P, 2, D])
        yre = place(74 * KB, "yre", [P, 2, D])
        yim = place(82 * KB, "yim", [P, 2, D])
        yt = place(90 * KB, "yt", [P, 2, 2, 512])
        yhy = place(66 * KB, "yhy", [P, KD, T])
        tT = place(50 * KB, "tT", [P, KD, T])
        tda = place(58 * KB, "tda", [P, 4, T])

        ps = ctx.enter_context(nc.psum_tensor("ps", [P, 8, 512], F32))

        def cc(name, n=1):
            return con[:, CC[name]:CC[name] + n]

        def pc(name, k=0, n=1):
            return par[:, COL[name] + k:COL[name] + k + n]

        ones, ident, tri = cc("ones", P), cc("ident", P), cc("tri", P)
        STAT, ADA = 4, 7
        raw_landed = [sem(f"raw_landed{r}") for r in range(RAW)]
        hi_done, lo_done, slab_used = sem("hi_done"), sem("lo_done"), sem("slab_used")
        bank_free = [sem(f"bank_free{b}") for b in range(BANKS)]
        block = ctx.enter_context(nc.Block())

        def slab(st, i, c):
            return st.s0 + st.body * i + c

        def uses(st, i, oc):
            b = oc % BANKS
            per_trip = len([k for k in range(st.body // st.per_out) if k % BANKS == b])
            return st.uses0[b] + per_trip * i + oc // BANKS

        def ahead(st, i, c):
            if c + HL < st.body:
                return st, i, c + HL
            if isinstance(i, int) and i == st.trips - 1:
                return (st.next, 0, c + HL - st.body) if st.next else None
            return st, i + 1, c + HL - st.body

        def trips(eng, st, body):
            if st.trips == 2:
                body(0)
            elif st.trips > 2:
                with eng.Fori(0, st.trips - 1) as i:
                    body(i)
            body(st.trips - 1)

        def wait(eng, s, n):
            if not (isinstance(n, int) and n <= 0):
                eng.wait_ge(s, n)

        def drained(eng, st):
            for b in range(BANKS):
                wait(eng, bank_free[b], st.uses1[b])

        SPLIT = [m for m in NORMS if m[:3] in ("mix", "ffn", "pre", "mod")]
        UPDATE = [m for m in NORMS if m not in SPLIT]

        def norm_of(m):
            x, c = slice(0, T), slice(T, 2 * T)
            src, cols = xT, (c if m[-2:] == "2c" else x)
            if m[:4] == "post":
                src, cols = proj, (c if m == "post_mix2" else cols)
            gain = {"mix1": lambda k: pc("norm_mix", k), "ffn1": lambda k: pc("norm_ffn", k),
                    "final1": lambda k: pc("norm_final", k)}.get(m)
            if gain is None:
                row = ["pre2x", "pre2c", "post2x", "post2c", "mod2x", "mod2c", "post_mix2", "pre3",
                       "post3"].index(m)
                gain = lambda k: gmod[:, row, k:k + 1]
            q = {"pre2": 0, "mod2": 3, "pre3": 6}.get(m[:4])
            if q is None:
                shift = lambda k: cc("zero")
            else:
                shift = lambda k: mod[:, q, k, (1 if m[-1] == "c" else 0):(2 if m[-1] == "c" else 1)]
            return src, cols, gain, shift

        @block.sync
        def _(sp):
            sp.dma_start(xT[:, :, 0:T], d["x"]).then_inc(sem("x_landed"), 16)
            sp.dma_start(con[:, :], d["consts"]).then_inc(sem("con_landed"), 16)
            sp.dma_start(par[:, :], d["params"]).then_inc(sem("par_landed"), 16)

            def load(st, i, c):
                r = (st.s0 + c) % RAW
                wait(sp, lo_done, slab(st, i, c) - RAW + 1)
                sp.dma_start(raw[:, r, 0:st.kt * P], d[st.weights][st.first + st.body * i + c])\
                  .then_inc(raw_landed[r], 16)

            for st in order:
                if st.name == "hy_v":
                    sp.wait_ge(slab_used, stages["hy_x1"].s0 + 1)
                    sp.dma_start(rope[:, :, :], d["rope"]).then_inc(sem("rope_landed"), 16)
                    sp.dma_start(dft[:, :, :], d["dft"]).then_inc(sem("dft_landed"), 16)
                    sp.dma_start(zT[:, :], d["filt_z"]).then_inc(sem("z_landed"), 16)
                if st.trips == 1:
                    for c in range(st.body):
                        load(st, 0, c)
                else:
                    with sp.Fori(0, st.trips) as i:
                        for c in range(st.body):
                            load(st, i, c)
            sp.wait_ge(sem("x_updated"), 8 * len(UPDATE))
            sp.dma_start(out, xT[:, :, 0:T]).then_inc(sem("out_landed"), 16)
            sp.wait_ge(sem("out_landed"), 16)

        @block.gpsimd
        def _(pool):
            for r in range(4):
                pool.dma_start(ada[:, r, :], d["w_ada"][r]).then_inc(sem(f"ada_landed{r}"), 16)

            def load_ada(n, r):
                pool.wait_ge(sem("ada_used"), n - 3)
                pool.dma_start(ada[:, r, :], d["w_ada"][n]).then_inc(sem(f"ada_landed{r}"), 16)

            with pool.Fori(1, 4) as i:
                for r in range(4):
                    load_ada(4 * i + r, r)
            for b in range(BANKS):
                pool.wait_ge(bank_free[b], stages["in1"].uses1[b])
            pool.wait_ge(sem("rcount_landed"), 16)
            n = 0

            def step(ins):
                nonlocal n
                n += 1
                ins.then_inc(sem("pool_step"), 1)
                pool.wait_ge(sem("pool_step"), n)

            sums = [u1[:, POOL1:POOL1 + 2, :], pools[:, 0:2, :], pools[:, 2:4, :],
                    pools[:, 4:5, :], pools[:, 5:6, :]]
            for lvl in range(4):
                w, a, to = 1 << lvl, sums[lvl], sums[lvl + 1]
                if lvl == 2:
                    a = a[:, 1:2, :]
                step(pool.tensor_tensor(to[:, :, w:T], a[:, :, w:T], a[:, :, 0:T - w], ALU.add))
                step(pool.tensor_copy(to[:, :, 0:w], a[:, :, 0:w]))
            for g, s in enumerate((pools[0:64, 0, :], pools[64:128, 2, :], pools[0:64, 4, :],
                                   pools[64:128, 5, :])):
                h0, tl = 64 * (g % 2), g // 2
                step(pool.tensor_tensor(s, s, rcount[h0:h0 + 64, tl, :], ALU.mult))
                pool.tensor_tensor(pools[h0:h0 + 64, tl, :], s, u1[h0:h0 + 64, POOL1 + tl, :],
                                   ALU.subtract).then_inc(sem("pool_in_ready"), 1)
            for c in range(12):
                load_ada(16 + c, c % 4)
            with pool.Fori(7, 18) as i:
                for r in range(4):
                    load_ada(4 * i + r, r)

        @block.scalar
        def _(act):
            act.dma_start(act_c[:, :, :], d["cvec"]).then_inc(sem("c_landed"), 16)
            act.dma_start(rcount[:, :, :], d["rcount"]).then_inc(sem("rcount_landed"), 16)
            act.dma_start(poolw[:, :, :], d["pool_w"]).then_inc(sem("poolw_landed"), 16)
            act.dma_start(xT[:, :, T:2 * T], d["ctx"]).then_inc(sem("ctx_landed"), 16)

            def split(st, i, c):
                s, r, h, n = slab(st, i, c), (st.s0 + c) % RAW, (st.s0 + c) % HL, st.kt * P
                lap = (st.s0 + c) // RAW + (i if st.body == RAW else 0)
                act.wait_ge(raw_landed[r], 16 * lap + 16)
                wait(act, slab_used, s - HL + 1)
                act.activation(hi[:, h, 0:n], raw[:, r, 0:n], ACT.Copy).then_inc(hi_done, 1)

            def epilogue(st, i, c):
                oc, col, kind = c // st.per_out, st.body * i + c, st.name
                if (c + 1) % st.per_out:
                    return
                b = oc % BANKS
                got = ps[:, b, 0:st.cols]
                n_used = slab(st, i, c) + 1
                if kind == "in1_head" or kind == "in1":
                    act.wait_ge(slab_used, n_used)
                    to = u1[:, 16 + c, :] if kind == "in1_head" else u1[:, col, :]
                    act.activation(to, got, ACT.Copy).then_inc(bank_free[b], 1)
                elif kind[:2] == "up":
                    q = c // 2
                    sg, pr, hh = (sg2, pr2, hh2) if st.cols > T else (sg1, pr1, hh1)
                    if c % 2 == 0:
                        act.wait_ge(slab_used, n_used)
                        act.activation(sg[:, q, :], got, ACT.Silu).then_inc(bank_free[b], 1)
                    else:
                        act.wait_ge(bank_free[b], uses(st, i, oc) + 1)
                        act.activation(hh[:, 2 * i + q, :], pr[:, q, :], ACT.Copy)\
                           .then_inc(sem("hh_done"), 1)
                elif kind in ("down2", "down3", "o2"):
                    act.wait_ge(slab_used, n_used)
                    j = (st.body // st.per_out) * i + oc
                    o = T if kind == "o2" else 0
                    act.activation(proj[:, j, o:o + st.cols], got, ACT.Copy).then_inc(bank_free[b], 1)
                elif kind[:3] == "hy_" and kind != "hy_out":
                    act.wait_ge(slab_used, n_used)
                    to = cvt[:, c, :] if kind == "hy_v" else (u if kind == "hy_x1" else x0)[:, col, :]
                    j = st.first + col
                    act.activation(to, got, ACT.Identity,
                                   scale=par[:, bass.ds(COL["hy_w"] + 24 + j, 1)],
                                   bias=par[:, bass.ds(COL["hy_b"] + j, 1)])\
                       .then_inc(sem("conv_mid"), 1)
                elif kind == "k2":
                    act.wait_ge(slab_used, n_used)
                    act.activation(kT[:, col, T:2 * T], ps[:, b, T:2 * T], ACT.Copy)\
                       .then_inc(sem("k_ctx_done"), 1)
                elif kind == "v2":
                    act.wait_ge(slab_used, n_used)
                    act.activation(V[:, :, bass.ds(P * col, P)],
                                   ps[:, b, :].rearrange("p (t n) -> p t n", t=4), ACT.Copy)\
                       .then_inc(bank_free[b], 1)
                elif kind == "gate2":
                    act.wait_ge(slab_used, n_used)
                    act.activation(gT[:, col, :], got, ACT.Sigmoid).then_inc(bank_free[b], 1)

            def stage(name):
                st = stages[name]

                def body(i):
                    for c in range(st.body):
                        nxt = ahead(st, i, c)
                        if nxt:
                            split(*nxt)
                        epilogue(st, i, c)

                trips(act, st, body)

            def norm(m):
                n = NORMS.index(m)
                src, cols, _, shift = norm_of(m)
                act.activation(sq[:, :, :], src[:, :, cols], ACT.Square).then_inc(sem("sq_ready"), 1)
                act.wait_ge(sem("stat_ready"), n + 1)
                wait(act, sem("rinv_ready"), n)
                act.activation(rtmp[:, :], ps[:, STAT, 0:T], ACT.Sqrt, scale=1.0 / D,
                               bias=cc("eps")).then_inc(sem("root_ready"), 1)
                if m in SPLIT:
                    s = SPLIT.index(m)
                    for k in range(KD):
                        act.wait_ge(sem("xg_ready"), 8 * s + k + 1)
                        act.activation(nh[:, k, cols], xg[:, k, :], ACT.Identity, bias=shift(k))\
                           .then_inc(sem("nh_ready"), 1)

            def updated(m):
                act.wait_ge(sem("x_updated"), 8 * (UPDATE.index(m) + 1))

            act.wait_ge(sem("c_landed"), 16)
            act.activation(act_c[:, :, :], act_c[:, :, :], ACT.Silu).then_inc(sem("c_ready"), 1)
            split(order[0], 0, 0)
            split(order[0], 0, 1)
            act.wait_ge(sem("x_landed"), 16)
            act.wait_ge(sem("con_landed"), 16)
            act.wait_ge(sem("par_landed"), 16)
            norm("mix1")
            stage("in1_head")
            stage("in1")

            act.activation(small[0:6, 0:1], pc("a_log")[0:6, :], ACT.Exp).then_inc(sem("a_ready"), 1)
            act.wait_ge(sem("dt_biased"), 1)
            act.activation(dtA[0:6, 3, :], dtA[0:6, 2, :], ACT.Abs).then_inc(sem("dt_step"), 1)
            act.wait_ge(sem("dt_step"), 1)
            act.activation(dtA[0:6, 3, :], dtA[0:6, 3, :], ACT.Exp, scale=-1.0).then_inc(sem("dt_step"), 1)
            act.wait_ge(sem("dt_step"), 2)
            act.activation(dtA[0:6, 3, :], dtA[0:6, 3, :], ACT.Ln, bias=cc("one")[0:6, :])\
               .then_inc(sem("dt_step"), 1)
            act.wait_ge(sem("vt_ready"), 1)
            act.activation(vtok[:, :, :], ps[:, 5:7, 0:384], ACT.Copy).then_inc(sem("vtok_copied"), 1)

            def out_pair(t):
                act.wait_ge(sem("o1_ready"), 2 * t + 2)
                act.activation(mixT[:, t, :], ps[:, 5 + t % 2, 0:T], ACT.Copy)\
                   .then_inc(sem("o1_copied"), 1)

            for h in range(HEADS1):
                r = h % 2
                act.wait_ge(sem("nmax_ready"), 2 * h + 2)
                if h >= 2:
                    act.wait_ge(sem("pt_ready"), h - 1)
                for qt, (a, b) in enumerate(((0, 128), (128, 384))):
                    act.activation(prob[:, r, a:b], scor[:, r, a:b], ACT.Exp,
                                   bias=small[:, 2 + 2 * h + qt:3 + 2 * h + qt],
                                   accum_out=small[:, 14 + 2 * h + qt:15 + 2 * h + qt])\
                       .then_inc(sem("prob_ready"), 1)
                act.wait_ge(sem("pt_ready"), h + 1)
                act.activation(pT[:, r, :], ps[:, 2 + r, 0:384], ACT.Copy).then_inc(sem("pt_copied"), 1)
                if h in (2, 4):
                    out_pair(h // 2 - 1)
            out_pair(2)

            act.wait_ge(sem("conv1_done"), 7)
            act.activation(cT[:, :, :], cT[:, :, :], ACT.Silu).then_inc(sem("cT_ready"), 1)
            act.activation(u1[:, Z1:Z1 + 3, :], u1[:, Z1:Z1 + 3, :], ACT.Silu).then_inc(sem("z_ready"), 1)
            act.wait_ge(sem("bt_ready"), 1)
            act.activation(btok[:, :, :], ps[:, STAT, 64:320].rearrange("p (g n) -> p g n", g=2),
                           ACT.Copy).then_inc(sem("btok_copied"), 1)
            act.wait_ge(sem("dte_arg"), 1)
            act.activation(small[:, 64:70], small[:, 64:70], ACT.Exp).then_inc(sem("dte_ready"), 1)
            act.wait_ge(sem("arow_ready"), 1)
            act.activation(CE[:, 0:2, :], ps[:, 1, 256:512].rearrange("p (a n) -> p a n", a=2),
                           ACT.Exp).then_inc(sem("ce_exp"), 1)
            act.activation(CE[:, 2:6, :], ps[:, 2, :].rearrange("p (a n) -> p a n", a=4),
                           ACT.Exp).then_inc(sem("ce_exp"), 1)
            act.wait_ge(sem("seg_ready"), 12)
            act.activation(seg[:, :, :], seg[:, :, :], ACT.Exp).then_inc(sem("decay1_ready"), 1)
            act.wait_ge(sem("prev_ready"), 1)
            act.activation(prev[:, :], ps[:, 5, 0:384], ACT.Copy).then_inc(sem("prev_copied"), 1)
            for t in range(2):
                act.wait_ge(sem("pool_ready"), 1)
                act.activation(mixT[:, 6 + t, :], ps[:, 6, t * T:t * T + T], ACT.Copy,
                               scale=pc("pool_scale", t)).then_inc(sem("pool_copied"), 1)
            act.wait_ge(sem("gated_ready"), 1)
            act.activation(ysq[:, :, :], yssd[:, :, :], ACT.Square).then_inc(sem("ysq_ready"), 1)
            act.wait_ge(sem("ystat_ready"), 1)
            act.activation(yroot[:, :, :], ps[:, 3:5, 0:T], ACT.Sqrt, scale=1.0 / 192, bias=cc("eps"))\
               .then_inc(sem("yroot_ready"), 1)
            act.wait_ge(sem("mix_ready"), 1)
            act.wait_ge(sem("o1_copied"), 3)
            act.wait_ge(sem("pool_copied"), 2)
            act.activation(nh[:, :, 0:T], mixT[:, :, :], ACT.Copy).then_inc(sem("mix_hi"), 1)

            stage("out1")
            drained(act, stages["out1"])
            norm("ffn1")
            stage("up1")
            stage("down1")
            drained(act, stages["down1"])
            act.wait_ge(sem("lam_dots"), 1)
            act.activation(small[:, 82:84], ps[:, 5, 0:2], ACT.Exp).then_inc(sem("lam_exp"), 1)
            norm("final1")
            updated("final1")
            norm("pre2x")
            act.wait_ge(sem("ctx_landed"), 16)
            norm("pre2c")
            stage("up2")
            stage("down2")
            drained(act, stages["down2"])
            norm("post2x")
            norm("post2c")
            updated("post2x")
            norm("mod2x")
            updated("post2c")
            norm("mod2c")
            for name in ("hy_x1", "hy_v", "hy_x0", "k2", "q2", "v2", "gate2"):
                stage(name)
            act.wait_ge(slab_used, stages["gate2"].s1)
            act.dma_start(decay[:, :, :], d["decay"]).then_inc(sem("decay_landed"), 16)
            act.dma_start(w4[:, :], d["filt_w4"]).then_inc(sem("w4_landed"), 16)

            def move_head(r):
                act.wait_ge(sem("pt2_ready"), r + 1)
                act.activation(pT2[:, r % 2, :, :], ps[:, 4 + r % 2, :].rearrange("p (k q) -> p k q", k=4),
                               ACT.Copy).then_inc(sem("pt2_copied"), 1)

            def take_out(r):
                act.wait_ge(sem("o2_ready"), r + 1)
                act.activation(otok[:, r, :], ps[:, 6 + r % 2, 0:P], ACT.Copy).then_inc(sem("otok_ready"), 1)

            for r in range(2 * HEADS2):
                act.wait_ge(sem("nmax2_ready"), r + 1)
                if r >= 2:
                    act.wait_ge(sem("pt2_ready"), r - 1)
                for m in range(2):
                    act.activation(p2[:, r % 2, m, :], ps[:, 2 * (r % 2) + m, :], ACT.Exp,
                                   scale=0.125, bias=small[:, 96 + 2 * r + m:97 + 2 * r + m],
                                   accum_out=small[:, 128 + 2 * r + m:129 + 2 * r + m])\
                       .then_inc(sem("prob2_ready"), 1)
                if r >= 1:
                    move_head(r - 1)
                if r >= 2:
                    take_out(r - 2)
            move_head(2 * HEADS2 - 1)
            take_out(2 * HEADS2 - 2)
            take_out(2 * HEADS2 - 1)

            for n in range(3):
                act.wait_ge(sem("sin_arg"), n + 1)
                act.activation(filt[:, 4, :], filt[:, 3, :], ACT.Sin).then_inc(sem("sin_ready"), 1)
            act.wait_ge(sem("hfb_ready"), 8)
            act.activation(absk[:, :, :], hfb[:, :, :], ACT.Abs).then_inc(sem("abs_ready"), 1)

            for g in range(4):
                tt, half = g // 2, g % 2
                act.wait_ge(sem("ut_ready"), g + 1)
                if g == 0:
                    act.wait_ge(sem("hsd_ready"), 2)
                act.activation(utok[:, tt, half * 512:half * 512 + 512], ps[:, g, :], ACT.Copy)\
                   .then_inc(sem("ut_copied"), 1)
            for g in range(8):
                to = kre if g < 4 else kim
                ft, half = g % 4 // 2, g % 2
                act.wait_ge(sem("kf_ready"), g + 1)
                act.activation(to[:, ft, half * 512:half * 512 + 512], ps[:, 4 + g % 4, :], ACT.Copy)\
                   .then_inc(sem("kf_copied"), 1)

            act.wait_ge(sem("oss_ready"), 2 * HEADS2)
            act.activation(small[:, 208:224], small[:, 192:208], ACT.Sqrt, scale=1.0 / P,
                           bias=cc("eps")).then_inc(sem("oroot_ready"), 1)
            for j in range(KD):
                act.wait_ge(sem("ott_ready"), j + 1)
                act.activation(nh[:, j, 0:T], ps[:, 4 + j % 4, 0:T], ACT.Copy, scale=small[:, 84:85])\
                   .then_inc(sem("o_hi"), 1)
            act.wait_ge(sem("yhy_ready"), KD)
            act.activation(nh[:, :, T:2 * T], yhy[:, :, :], ACT.Copy).then_inc(sem("yhy_hi"), 1)
            stage("da_out")
            stage("hy_out")
            act.wait_ge(sem("tT_ready"), KD)
            act.activation(nh[:, :, 0:T], tT[:, :, :], ACT.Copy).then_inc(sem("t_hi"), 1)
            stage("o2")
            drained(act, stages["o2"])
            norm("post_mix2")
            updated("post_mix2")
            norm("pre3")
            stage("up3")
            stage("down3")
            drained(act, stages["down3"])
            norm("post3")

        @block.vector
        def _(dve):
            n = 0

            def step(ins):
                nonlocal n
                n += 1
                ins.then_inc(sem("dve_step"), 1)
                return n

            def after(k):
                dve.wait_ge(sem("dve_step"), k)

            def split(st, i, c):
                s, r, h, w = slab(st, i, c), (st.s0 + c) % RAW, (st.s0 + c) % HL, st.kt * P
                dve.wait_ge(hi_done, s + 1)
                dve.tensor_tensor(lo[:, h, 0:w], raw[:, r, 0:w], hi[:, h, 0:w].bitcast(F32),
                                  ALU.subtract).then_inc(lo_done, 1)

            def short_taps(c, col, st, b, to):
                k = (stages["hy_x1"].s0, )[0]
                done = slab(st, 0, 0) - k + st.body * (col[0]) + c + 1
                dve.wait_ge(sem("conv_mid"), done)
                j = st.first + st.body * col[0] + c
                w0 = par[:, bass.ds(COL["hy_w"] + j, 1)]
                w2 = par[:, bass.ds(COL["hy_w"] + 48 + j, 1)]
                dve.scalar_tensor_tensor(to[:, 1:T], ps[:, b, 0:T - 1], w0, to[:, 1:T], ALU.mult,
                                         ALU.add).then_inc(sem("conv_left"), 1)
                dve.wait_ge(sem("conv_left"), done)
                return done, w2

            def epilogue(st, i, c):
                oc, col, kind = c // st.per_out, st.body * i + c, st.name
                if (c + 1) % st.per_out:
                    return
                b = oc % BANKS
                got = ps[:, b, 0:st.cols]
                n_used = slab(st, i, c) + 1
                if kind in ("out1", "down1"):
                    dve.wait_ge(slab_used, n_used)
                    j = (st.body // st.per_out) * i + oc
                    dve.tensor_tensor(xT[:, j, 0:T], xT[:, j, 0:T], got, ALU.add)\
                       .then_inc(bank_free[b], 1)
                elif kind[:3] == "hy_" and kind != "hy_out":
                    to = cvt[:, c, :] if kind == "hy_v" else (u if kind == "hy_x1" else x0)[:, col, :]
                    done, w2 = short_taps(c, (i,), st, b, to)
                    dve.scalar_tensor_tensor(to[:, 0:T - 1], ps[:, b, 1:T], w2, to[:, 0:T - 1],
                                             ALU.mult, ALU.add).then_inc(bank_free[b], 1)
                    if kind == "hy_v":
                        dve.wait_ge(bank_free[b], uses(st, i, oc) + 1)
                        dve.tensor_tensor(u[:, col, :], u[:, col, :], cvt[:, c, :], ALU.mult)\
                           .then_inc(sem("u_ready"), 1)
                elif kind in ("k2", "q2"):
                    base = 0 if kind == "k2" else 8
                    dve.wait_ge(slab_used, n_used)
                    if kind == "k2":
                        dve.wait_ge(sem("k_ctx_done"), col + 1)
                    part = rot[:, c % 2, 0, :]
                    same = rot[:, c % 2, 1, :]
                    dve.stream_shuffle(part, ps[:, b, 0:T], [(j + 16) % 32 for j in range(32)])\
                       .then_inc(sem("rot_part"), 1)
                    dve.tensor_tensor(same, ps[:, b, 0:T], rope[:, 0, :], ALU.mult)\
                       .then_inc(bank_free[b], 1)
                    dve.wait_ge(sem("rot_part"), base + col + 1)
                    dve.tensor_tensor(part, part, rope[:, 1, :], ALU.mult).then_inc(sem("rot_sin"), 1)
                    dve.wait_ge(sem("rot_sin"), base + col + 1)
                    to = kT if kind == "k2" else qT
                    dve.wait_ge(bank_free[b], uses(st, i, oc) + 1)
                    dve.tensor_tensor(to[:, col, 0:T], same, part, ALU.add).then_inc(sem("rot_done"), 1)
                elif kind == "da_out":
                    dve.wait_ge(slab_used, n_used)
                    dve.tensor_tensor(tT[:, col, :], gT[:, KD + col, :], got, ALU.mult)\
                       .then_inc(bank_free[b], 1)
                elif kind == "hy_out":
                    dve.wait_ge(slab_used, n_used)
                    dve.tensor_tensor(tda[:, c, :], gT[:, col, :], got, ALU.mult).then_inc(bank_free[b], 1)
                    dve.wait_ge(bank_free[b], uses(st, i, oc) + 1)
                    dve.tensor_tensor(tT[:, col, :], tT[:, col, :], tda[:, c, :], ALU.add)\
                       .then_inc(sem("tT_ready"), 1)

            def stage(name):
                st = stages[name]
                sg, pr, hh, hl = (sg2, pr2, hh2, hl2) if st.cols > T else (sg1, pr1, hh1, hl1)

                def body(i):
                    for c in range(st.body):
                        q = c // 2
                        if name[:2] == "up" and c % 2:
                            dve.wait_ge(bank_free[c - 1], uses(st, i, c - 1) + 1)
                            dve.wait_ge(slab_used, slab(st, i, c) + 1)
                            dve.tensor_tensor(pr[:, q, :], sg[:, q, :], ps[:, c, 0:st.cols], ALU.mult)\
                               .then_inc(bank_free[c], 1)
                        nxt = ahead(st, i, c)
                        if nxt:
                            split(*nxt)
                        if name[:2] == "up" and c % 2:
                            dve.wait_ge(sem("hh_done"), pairs_before(name) + 2 * i + q + 1)
                            dve.tensor_tensor(hl[:, 2 * i + q, :], pr[:, q, :],
                                              hh[:, 2 * i + q, :].bitcast(F32), ALU.subtract)\
                               .then_inc(sem("hl_done"), 1)
                        epilogue(st, i, c)

                trips(dve, st, body)

            def norm(m):
                k0 = NORMS.index(m)
                src, cols, gain, shift = norm_of(m)
                dve.wait_ge(sem("root_ready"), k0 + 1)
                dve.reciprocal(rinv[:, :], rtmp[:, :]).then_inc(sem("rinv_ready"), 1)
                dve.wait_ge(sem("rinv_ready"), k0 + 1)
                if m == "final1":
                    for k in range(KD):
                        dve.scalar_tensor_tensor(xT[:, k, 0:T], xT[:, k, 0:T], gain(k), rinv[:, :],
                                                 ALU.mult, ALU.mult).then_inc(sem("x_updated"), 1)
                    return
                if m in UPDATE:
                    to = slice(T, 2 * T) if m[-1] == "c" else slice(0, T)
                    ks = []
                    for k in range(KD):
                        ks.append(step(dve.scalar_tensor_tensor(
                            xg[:, k, :], proj[:, k, cols], gain(k), rinv[:, :], ALU.mult, ALU.mult)))
                    for k in range(KD):
                        after(ks[k])
                        dve.tensor_tensor(xT[:, k, to], xT[:, k, to], xg[:, k, :], ALU.add)\
                           .then_inc(sem("x_updated"), 1)
                    return
                for k in range(KD):
                    dve.scalar_tensor_tensor(xg[:, k, :], src[:, k, cols], gain(k), rinv[:, :],
                                             ALU.mult, ALU.mult).then_inc(sem("xg_ready"), 1)
                s = SPLIT.index(m)
                for k in range(KD):
                    dve.wait_ge(sem("nh_ready"), 8 * s + k + 1)
                    dve.scalar_tensor_tensor(nl[:, k, cols], xg[:, k, :], shift(k),
                                             nh[:, k, cols].bitcast(F32), ALU.add, ALU.subtract)\
                       .then_inc(sem("nl_ready"), 1)

            dve.memset(small[:, :], 0.0).then_inc(sem("dve_step"), 1)
            n = 1
            split(order[0], 0, 0)
            split(order[0], 0, 1)
            dve.wait_ge(sem("x_landed"), 16)
            dve.wait_ge(sem("par_landed"), 16)
            dve.wait_ge(sem("con_landed"), 16)
            norm("mix1")
            stage("in1_head")
            stage("in1")

            drained(dve, stages["in1"])
            dve.tensor_scalar(dtA[0:6, 2, :], u1[0:6, DT1, :], pc("dt_bias")[0:6, :], None, ALU.add)\
               .then_inc(sem("dt_biased"), 1)
            dve.wait_ge(sem("dt_step"), 3)
            k1 = step(dve.scalar_tensor_tensor(dtA[0:6, 0, :], dtA[0:6, 2, :], 0.0, dtA[0:6, 3, :],
                                               ALU.max, ALU.add))
            after(k1)
            dve.wait_ge(sem("a_ready"), 1)
            dve.tensor_scalar(dtA[0:6, 1, :], dtA[0:6, 0, :], small[0:6, 0:1], -1.0, ALU.mult, ALU.mult)\
               .then_inc(sem("dtA_ready"), 1)
            dve.wait_ge(sem("dtok_ready"), 1)
            k1 = step(dve.tensor_copy(small[:, 160:184], ps[:, STAT, 0:24]))
            after(k1)
            dve.wait_ge(sem("con_landed"), 16)
            for j in range(12):
                ch, h = j // 6, j % 6
                o = 160 + 12 * ch + 6 + h
                dve.tensor_scalar(triA[:, j, :], tri, small[:, o:o + 1], None, ALU.mult)\
                   .then_inc(sem("triA_ready"), 1)

            def conv_tile(j):
                src = u1[:, XBC1 + j, :]
                k = step(dve.tensor_scalar(cT[:, j, :], src, pc("conv_w", 21 + j), pc("conv_b", j),
                                           ALU.mult, ALU.add))
                for lag in (1, 2, 3):
                    after(k)
                    ins = dve.scalar_tensor_tensor(cT[:, j, lag:T], src[:, 0:T - lag],
                                                   pc("conv_w", 7 * (3 - lag) + j), cT[:, j, lag:T],
                                                   ALU.mult, ALU.add)
                    if lag < 3:
                        k = step(ins)
                ins.then_inc(sem("conv1_done"), 1)

            for h in range(HEADS1):
                r = h % 2
                dve.wait_ge(sem("scores_ready"), h + 1)
                if h >= 2:
                    dve.wait_ge(sem("prob_ready"), 2 * h - 2)
                dve.scalar_tensor_tensor(scor[:, r, :], ps[:, r, 0:384], 0.125, cc("mask384", 384),
                                         ALU.mult, ALU.add).then_inc(sem("scores_masked"), 1)
                dve.wait_ge(sem("scores_masked"), h + 1)
                for qt, (a, b) in enumerate(((0, 128), (128, 384))):
                    o = 2 + 2 * h + qt
                    dve.tensor_reduce(small[:, o:o + 1], scor[:, r, a:b], AX.X, ALU.max, negate=True)\
                       .then_inc(sem("nmax_ready"), 1)
                conv_tile(h)
                dve.wait_ge(sem("prob_ready"), 2 * h + 2)
                o = 14 + 2 * h
                k = step(dve.reciprocal(small[:, o + 12:o + 14], small[:, o:o + 2]))
                after(k)
                for qt, (a, b) in enumerate(((0, 128), (128, 384))):
                    dve.tensor_scalar(prob[:, r, a:b], prob[:, r, a:b],
                                      small[:, o + 12 + qt:o + 13 + qt], None, ALU.mult)\
                       .then_inc(sem("prob_scaled"), 1)
            conv_tile(6)

            def dtok(ch, kind):
                o = 160 + 12 * ch + 6 * kind
                return small[:, o:o + 6]

            dve.wait_ge(sem("xs_ready"), 1)
            for ch in range(2):
                dve.tensor_tensor(xdt[:, ch, :].rearrange("p (h d) -> p h d", h=6),
                                  ps[:, 5 + ch, 0:384].rearrange("p (h d) -> p h d", h=6),
                                  dtok(ch, 0).unsqueeze(2).broadcast_to([P, 6, 64]), ALU.mult)\
                   .then_inc(sem("xdt_ready"), 1)
            dve.wait_ge(sem("acum_ready"), 1)
            k = step(dve.tensor_copy(small[:, 40:64], ps[:, STAT, 32:56]))
            after(k)
            dve.tensor_tensor(small[:, 64:70], small[:, 52:58], small[:, 40:46], ALU.subtract)\
               .then_inc(sem("dte_arg"), 1)
            dve.wait_ge(sem("arow_ready"), 1)
            for j in range(12):
                ch, h = j // 6, j % 6
                if j == 4:
                    dve.wait_ge(sem("ce_exp"), 2)
                dve.scalar_tensor_tensor(seg[:, j, :], ps[:, j // 4, (j % 4) * P:(j % 4) * P + P],
                                         small[:, 40 + 6 * ch + h:41 + 6 * ch + h], cc("maskT", P),
                                         ALU.subtract, ALU.add).then_inc(sem("seg_ready"), 1)
            dve.wait_ge(sem("dte_ready"), 1)
            dve.wait_ge(sem("xdt_ready"), 2)
            dve.tensor_tensor(xw[:, :].rearrange("p (h d) -> p h d", h=6),
                              xdt[:, 0, :].rearrange("p (h d) -> p h d", h=6),
                              small[:, 64:70].unsqueeze(2).broadcast_to([P, 6, 64]), ALU.mult)\
               .then_inc(sem("xw_ready"), 1)
            dve.wait_ge(sem("ce_exp"), 2)
            for g in range(2):
                dve.tensor_tensor(CE[:, 3 * g:3 * g + 3, :], CE[:, 3 * g:3 * g + 3, :],
                                  cT[:, 5 + g, P:2 * P].unsqueeze(1).broadcast_to([P, 3, P]), ALU.mult)\
                   .then_inc(sem("ce_ready"), 1)
            dve.wait_ge(sem("g_ready"), 1)
            dve.wait_ge(sem("decay1_ready"), 1)
            for j in range(4):
                dve.tensor_tensor(seg[:, 3 * j:3 * j + 3, :], seg[:, 3 * j:3 * j + 3, :],
                                  ps[:, 3, j * P:j * P + P].unsqueeze(1).broadcast_to([P, 3, P]), ALU.mult)\
                   .then_inc(sem("m_ready"), 1)
            dve.wait_ge(sem("y1_ready"), 1)
            dve.wait_ge(sem("z_ready"), 1)
            for t in range(3):
                k = step(dve.scalar_tensor_tensor(yssd[:, t, :], cT[:, t, :], pc("d_skip", t),
                                                  ps[:, t, 0:T], ALU.mult, ALU.add))
            after(k)
            dve.tensor_tensor(yssd[:, :, :], yssd[:, :, :], u1[:, Z1:Z1 + 3, :], ALU.mult)\
               .then_inc(sem("gated_ready"), 1)
            dve.wait_ge(sem("yroot_ready"), 1)
            dve.reciprocal(yrg[:, :, :], yroot[:, :, :]).then_inc(sem("yrg_ready"), 1)
            dve.wait_ge(sem("yrg_ready"), 1)
            for t, a, b, g in ((0, 0, 128, 0), (1, 0, 64, 0), (1, 64, 128, 1), (2, 0, 128, 1)):
                ins = dve.scalar_tensor_tensor(mixT[a:b, 3 + t, :], yssd[a:b, t, :],
                                               pc("ssd_norm", t)[a:b, :], yrg[a:b, g, :],
                                               ALU.mult, ALU.mult)
                if t < 2:
                    step(ins)
            ins.then_inc(sem("mix_ready"), 1)
            dve.wait_ge(sem("mix_hi"), 1)
            dve.tensor_tensor(nl[:, :, 0:T], mixT[:, :, :], nh[:, :, 0:T].bitcast(F32), ALU.subtract)\
               .then_inc(sem("mix_lo"), 1)

            stage("out1")
            norm("ffn1")
            stage("up1")

            dve.wait_ge(sem("ada_used"), 72)
            k = step(dve.tensor_tensor(mod[:, :, :, :].rearrange("p q k s -> p (q k) s"),
                                       ps[:, ADA, 0:144].rearrange("p (n s) -> p n s", s=2),
                                       pc("b_ada", 0, 72).unsqueeze(2).broadcast_to([P, 72, 2]), ALU.add))
            after(k)

            def gn(r):
                return pc("norm_g", 8 * r, 8)

            for row, q, s, g, kind in ((0, 1, 0, 0, "scale"), (1, 1, 1, 0, "scale"), (2, 2, 0, 1, "half"),
                                       (3, 2, 1, 1, "half"), (4, 4, 0, 2, "scale"), (5, 4, 1, 2, "scale"),
                                       (6, 5, 0, 3, "gate"), (7, 7, 0, 4, "scale"), (8, 8, 0, 5, "half")):
                k = step(dve.scalar_tensor_tensor(
                    gmod[:, row, :], mod[:, q, :, s], {"scale": 1.0, "half": 0.5, "gate": 1.0}[kind],
                    gn(g), ALU.add if kind == "scale" else ALU.mult, ALU.mult))
            dve.tensor_tensor(small[0:64, 80:82], pc("lam_q", 0, 2)[0:64, :], pc("lam_k", 0, 2)[0:64, :],
                              ALU.mult).then_inc(sem("lam_prod"), 1)
            k = step(dve.tensor_scalar(small[:, 84:85], pc("subln"), 1.0 - LAM_INIT, None, ALU.mult))
            after(k)
            stage("down1")
            dve.wait_ge(sem("lam_exp"), 1)
            k = step(dve.tensor_tensor(small[:, 85:86], small[:, 83:84], small[:, 82:83], ALU.subtract))
            after(k)
            k = step(dve.tensor_scalar(small[:, 86:87], small[:, 85:86], LAM_INIT, None, ALU.subtract))
            after(k)
            nlam = small[:, 86:87]
            norm("final1")
            norm("pre2x")
            norm("pre2c")
            stage("up2")
            stage("down2")
            for m in ("post2x", "post2c", "mod2x", "mod2c"):
                norm(m)
            for name in ("hy_x1", "hy_v", "hy_x0"):
                stage(name)
            dve.wait_ge(sem("rope_landed"), 16)
            for name in ("k2", "q2", "v2", "gate2"):
                stage(name)

            def mix_maps(r):
                a, b = p2[:, r % 2, 0, :], p2[:, r % 2, 1, :]
                dve.wait_ge(sem("prob2_ready"), 2 * r + 2)
                if r:
                    dve.wait_ge(sem("pmix_ready"), r)
                o = 128 + 2 * r
                k = step(dve.reciprocal(small[:, 224:226], small[:, o:o + 2]))
                after(k)
                k = step(dve.tensor_tensor(small[:, 226:227], small[:, 225:226], nlam, ALU.mult))
                after(k)
                k = step(dve.tensor_scalar(b, b, small[:, 226:227], None, ALU.mult))
                after(k)
                dve.scalar_tensor_tensor(a, a, small[:, 224:225], b, ALU.mult, ALU.add)\
                   .then_inc(sem("pmix_ready"), 1)

            def square_sum(r):
                dve.wait_ge(sem("otok_ready"), r + 1)
                if r >= 1:
                    dve.wait_ge(sem("oss_ready"), r)
                dve.tensor_tensor_reduce(out=rtmp[:, 0:P], in0=otok[:, r, :], in1=otok[:, r, :], scale=1.0,
                                         scalar=0.0, op0=ALU.mult, op1=ALU.add,
                                         accum_out=small[:, 192 + r:193 + r]).then_inc(sem("oss_ready"), 1)

            for r in range(2 * HEADS2):
                dve.wait_ge(sem("s2_ready"), r + 1)
                k = step(dve.tensor_reduce(small[:, 228 + 2 * (r % 2):230 + 2 * (r % 2)],
                                           ps[:, 2 * (r % 2):2 * (r % 2) + 2, :], AX.X, ALU.max))
                after(k)
                dve.tensor_scalar(small[:, 96 + 2 * r:98 + 2 * r],
                                  small[:, 228 + 2 * (r % 2):230 + 2 * (r % 2)], -0.125, None, ALU.mult)\
                   .then_inc(sem("nmax2_ready"), 1)
                if r >= 1:
                    mix_maps(r - 1)
                if r >= 3:
                    square_sum(r - 3)
            mix_maps(2 * HEADS2 - 1)
            for r in range(2 * HEADS2 - 3, 2 * HEADS2):
                square_sum(r)

            two_pi = 2.0 * np.pi
            c1 = float(np.float32(6.28125))
            c2 = float(np.float32(two_pi - c1))
            c3 = float(two_pi - c1 - c2)
            magic = 1.5 * 2.0 ** 23
            for l in range(3):
                dve.wait_ge(sem("filt_pre"), l + 1)
                x, t, y = filt[:, 0, :], filt[:, 1, :], filt[:, 2, :]
                k = step(dve.tensor_scalar(x, ps[0:64, 6, 0:T], pc("filt_b", l)[0:64, :],
                                           pc("filt_freq")[0:64, :], ALU.add, ALU.mult))
                after(k)
                k = step(dve.tensor_scalar(t, x, 1.0 / two_pi, magic, ALU.mult, ALU.add))
                after(k)
                k = step(dve.tensor_scalar(t, t, magic, None, ALU.subtract))
                after(k)
                k = step(dve.scalar_tensor_tensor(y, t, -c1, x, ALU.mult, ALU.add))
                after(k)
                k = step(dve.scalar_tensor_tensor(x, t, -c2, y, ALU.mult, ALU.add))
                after(k)
                k = step(dve.scalar_tensor_tensor(y, t, -c3, x, ALU.mult, ALU.add))
                after(k)
                pi = float(np.float32(3.1415925))
                dve.tensor_scalar(filt[:, 3, :], y, pi, -pi, ALU.min, ALU.max).then_inc(sem("sin_arg"), 1)
            dve.wait_ge(sem("decay_landed"), 16)
            for g in range(8):
                lt, q = g // 4, g % 4
                dve.wait_ge(sem("h_ready"), g + 1)
                ins = dve.tensor_tensor(hfb[:, lt, q * 512:q * 512 + 512], ps[:, g % 4, :],
                                        decay[:, lt, (q % 2) * 512:(q % 2) * 512 + 512], ALU.mult)
                if (lt, q) == (0, 3):
                    k = step(ins)
                    after(k)
                    ins = dve.memset(hfb[0:1, 0, D:2 * D], 0.0)
                ins.then_inc(sem("hfb_ready"), 1)
            dve.wait_ge(sem("hfb_ready"), 8)
            for s, op in enumerate((ALU.add, ALU.subtract)):
                dve.tensor_tensor(hsd[:, :, s * D:s * D + D], hfb[:, :, 0:D], hfb[:, :, D:2 * D], op)\
                   .then_inc(sem("hsd_ready"), 1)
            dve.wait_ge(sem("ksum_ready"), 1)
            dve.tensor_scalar(small[:, 232:240], ps[:, 6, 256:264], EPS, None, ALU.add)\
               .then_inc(sem("knorm_read"), 1)
            dve.wait_ge(sem("knorm_read"), 1)
            knorm = small[:, 240:248]
            k = step(dve.reciprocal(knorm, small[:, 232:240]))
            after(k)

            dve.wait_ge(sem("kf_copied"), 8)
            for g in range(4):
                ft, half = g // 2, g % 2
                w = slice(half * 512, half * 512 + 512)
                ur, ui = ps[:, 2 * (g % 2), :], ps[:, 2 * (g % 2) + 1, :]
                dve.wait_ge(sem("uf_ready"), g + 1)
                t0, t1 = yt[:, g % 2, 0, :], yt[:, g % 2, 1, :]
                k1 = step(dve.tensor_tensor(t0, kre[:, ft, w], ur, ALU.mult))
                k2 = step(dve.tensor_tensor(t1, kim[:, ft, w], ui, ALU.mult))
                after(k2)
                k3 = step(dve.tensor_tensor(yre[:, ft, w], t0, t1, ALU.subtract))
                after(k3)
                k4 = step(dve.tensor_tensor(t0, kim[:, ft, w], ur, ALU.mult))
                k5 = step(dve.tensor_tensor(t1, kre[:, ft, w], ui, ALU.mult))
                after(k5)
                dve.tensor_tensor(yim[:, ft, w], t0, t1, ALU.add).then_inc(sem("yf_ready"), 1)
            dve.wait_ge(sem("oroot_ready"), 1)
            k = step(dve.reciprocal(small[:, 144:160], small[:, 208:224]))
            after(k)
            dve.tensor_tensor(otok[:, :, :], otok[:, :, :],
                              small[:, 144:160].unsqueeze(2).broadcast_to([P, 2 * HEADS2, P]), ALU.mult)\
               .then_inc(sem("otok_scaled"), 1)
            for j in range(KD):
                k = step(dve.tensor_scalar(yt[:, j % 2, 0, 0:T], u[:, j, :], pc("hy_bias", j), None, ALU.mult))
                dve.wait_ge(sem("yc_ready"), j + 1)
                after(k)
                k = step(dve.scalar_tensor_tensor(yt[:, j % 2, 1, 0:T], ps[:, j % 4, 0:T],
                                                  knorm[:, j:j + 1], yt[:, j % 2, 0, 0:T], ALU.mult, ALU.add))
                after(k)
                dve.tensor_tensor(yhy[:, j, :], yt[:, j % 2, 1, 0:T], x0[:, j, :], ALU.mult)\
                   .then_inc(sem("yhy_ready"), 1)
            for j in range(KD):
                dve.wait_ge(sem("o_hi"), j + 1)
                dve.scalar_tensor_tensor(nl[:, j, 0:T], ps[:, 4 + j % 4, 0:T], small[:, 84:85],
                                         nh[:, j, 0:T].bitcast(F32), ALU.mult, ALU.subtract)\
                   .then_inc(sem("o_lo"), 1)
            dve.wait_ge(sem("yhy_hi"), 1)
            dve.tensor_tensor(nl[:, :, T:2 * T], yhy[:, :, :], nh[:, :, T:2 * T].bitcast(F32), ALU.subtract)\
               .then_inc(sem("yhy_lo"), 1)
            stage("da_out")
            stage("hy_out")
            dve.wait_ge(sem("t_hi"), 1)
            dve.tensor_tensor(nl[:, :, 0:T], tT[:, :, :], nh[:, :, 0:T].bitcast(F32), ALU.subtract)\
               .then_inc(sem("t_lo"), 1)
            stage("o2")
            norm("post_mix2")
            norm("pre3")
            stage("up3")
            stage("down3")
            norm("post3")

        @block.tensor
        def _(pe):
            mm = nc.tensor.matmul

            def dense(st, i, c, x_hi, x_lo, token_major=False):
                s, h = slab(st, i, c), (st.s0 + c) % HL
                oc, part = c // st.per_out, c % st.per_out
                b = oc % BANKS
                pe.wait_ge(lo_done, s + 1)
                if part == 0:
                    wait(pe, bank_free[b], uses(st, i, oc))
                for tt in range(st.cols // P if token_major else 1):
                    for k in range(st.kt):
                        wk = slice(k * P, k * P + P)
                        kk = part * st.kt + k
                        first = part == 0 and k == 0
                        last = part == st.per_out - 1 and k == st.kt - 1
                        if token_major:
                            tk = slice(tt * P, tt * P + P)
                            o = ps[:, b, tk]
                            mm(o, x_hi[:, kk, tk], hi[:, h, wk], start=first, stop=False)
                            mm(o, x_hi[:, kk, tk], lo[:, h, wk], start=False, stop=False)
                            m = mm(o, x_lo[:, kk, tk], hi[:, h, wk], start=False, stop=last)
                        else:
                            o = ps[:, b, 0:st.cols]
                            mm(o, hi[:, h, wk], x_hi[:, kk, 0:st.cols], start=first, stop=False)
                            mm(o, hi[:, h, wk], x_lo[:, kk, 0:st.cols], start=False, stop=False)
                            m = mm(o, lo[:, h, wk], x_hi[:, kk, 0:st.cols], start=False, stop=last)
                m.then_inc(slab_used, 1)

            def stage(name, x_hi=nh, x_lo=nl, token_major=False, beside=None):
                st = stages[name]

                def body(i):
                    for c in range(st.body):
                        dense(st, i, c, x_hi, x_lo, token_major)
                        if beside:
                            beside(i, c)

                if st.trips == 1:
                    body(0)
                else:
                    with pe.Fori(0, st.trips) as i:
                        body(i)

            def modulation(n, r):
                pe.wait_ge(sem(f"ada_landed{r}"), 16 * (n // 4 + 1) if isinstance(n, int) else n[0])
                at = 2 * n if isinstance(n, int) else n[1]
                for k in range(KD):
                    m = mm(ps[:, ADA, bass.ds(at, 2)], ada[:, r, k * P:k * P + P], act_c[:, k, :],
                           start=(k == 0), stop=(k == KD - 1))
                m.then_inc(sem("ada_used"), 1)

            def norm(m):
                n = NORMS.index(m)
                pe.wait_ge(sem("sq_ready"), n + 1)
                wait(pe, sem("root_ready"), n)
                for k in range(KD):
                    o = mm(ps[:, STAT, 0:T], ones, sq[:, k, :], start=(k == 0), stop=(k == KD - 1))
                o.then_inc(sem("stat_ready"), 1)

            def normed(m):
                pe.wait_ge(sem("nl_ready"), 8 * (SPLIT.index(m) + 1))

            pe.wait_ge(sem("con_landed"), 16)
            norm("mix1")
            normed("mix1")
            stage("in1_head")
            pe.wait_ge(sem("c_ready"), 1)
            stage("in1", beside=lambda i, c: modulation((16 * i + 16, 8 * i + 2 * c), c))

            drained(pe, stages["in1"])
            for tt in range(2):
                for j in range(NT1):
                    o = pe.transpose(ps[:, 5 + tt, j * P:j * P + P],
                                     u1[:, V1 + j, tt * P:tt * P + P], ident)
            o.then_inc(sem("vt_ready"), 1)

            def scores(h):
                t, a = h // 2, 64 * (h % 2)
                q, k = u1[a:a + 64, Q1 + t, :], u1[a:a + 64, K1 + t, :]
                if h >= 2:
                    pe.wait_ge(sem("scores_masked"), h - 1)
                mm(ps[:, h % 2, 0:P], q[:, 0:P], k[:, 0:P], start=True, stop=True)
                mm(ps[:, h % 2, P:3 * P], q[:, P:T], k[:, 0:T], start=True, stop=True)\
                    .then_inc(sem("scores_ready"), 1)

            def turn_probs(h):
                pe.wait_ge(sem("prob_scaled"), 2 * h + 2)
                if h >= 2:
                    pe.wait_ge(sem("pt_copied"), h - 1)
                for j in range(3):
                    o = pe.transpose(ps[:, 2 + h % 2, j * P:j * P + P],
                                     prob[:, h % 2, j * P:j * P + P], ident)
                o.then_inc(sem("pt_ready"), 1)

            def values(h):
                t, a = h // 2, 64 * (h % 2)
                pe.wait_ge(sem("pt_copied"), h + 1)
                if h == 0:
                    pe.wait_ge(sem("vtok_copied"), 1)
                if h == 4:
                    pe.wait_ge(sem("o1_copied"), 1)
                mm(ps[a:a + 64, 5 + t % 2, 0:T], vtok[:, 0, 64 * h:64 * h + 64], pT[:, h % 2, 0:T],
                   start=True, stop=False)
                mm(ps[a:a + 64, 5 + t % 2, P:T], vtok[:, 1, 64 * h:64 * h + 64], pT[:, h % 2, T:3 * P],
                   start=False, stop=True).then_inc(sem("o1_ready"), 1)

            scores(0)
            pe.wait_ge(sem("dtA_ready"), 1)
            for ch in range(2):
                for kind in range(2):
                    o = pe.transpose(ps[:, STAT, 12 * ch + 6 * kind:12 * ch + 6 * kind + 6],
                                     dtA[0:6, kind, ch * P:ch * P + P], ident[0:6, 0:6])
            o.then_inc(sem("dtok_ready"), 1)
            for h in range(HEADS1):
                if h + 1 < HEADS1:
                    scores(h + 1)
                for c in range(2 * h, 2 * h + 2):
                    modulation(16 + c, c % 4)
                turn_probs(h)
                if h >= 1:
                    values(h - 1)
            values(HEADS1 - 1)

            pe.wait_ge(sem("triA_ready"), 12)
            for ch in range(2):
                mm(ps[:, STAT, 32 + 6 * ch:38 + 6 * ch], tri, small[:, 166 + 12 * ch:172 + 12 * ch],
                   start=True, stop=True)
            for ch in range(2):
                o = mm(ps[:, STAT, 44 + 6 * ch:50 + 6 * ch], ones, small[:, 166 + 12 * ch:172 + 12 * ch],
                       start=True, stop=True)
            o.then_inc(sem("acum_ready"), 1)
            pe.wait_ge(sem("pt_copied"), HEADS1)
            pe.wait_ge(sem("scores_masked"), HEADS1)
            for b in range(3):
                o = mm(ps[:, b, :], ones, triA[:, 4 * b:4 * b + 4, :].rearrange("p a n -> p (a n)"),
                       start=True, stop=True)
            o.then_inc(sem("arow_ready"), 1)
            pe.wait_ge(sem("cT_ready"), 1)
            pe.wait_ge(sem("o1_copied"), 3)
            for tt in range(2):
                for j in range(NT1):
                    o = pe.transpose(ps[:, 5 + tt, j * P:j * P + P], cT[:, j, tt * P:tt * P + P], ident)
            o.then_inc(sem("xs_ready"), 1)
            pe.wait_ge(sem("dte_arg"), 1)
            for g in range(2):
                o = pe.transpose(ps[:, STAT, 64 + g * P:64 + g * P + P], cT[:, 3 + g, 0:P], ident)
            o.then_inc(sem("bt_ready"), 1)
            for ch in range(2):
                for g in range(2):
                    w = slice(ch * P, ch * P + P)
                    o = mm(ps[:, 3, (2 * ch + g) * P:(2 * ch + g) * P + P], cT[:, 3 + g, w],
                           cT[:, 5 + g, w], start=True, stop=True)
            o.then_inc(sem("g_ready"), 1)
            pe.wait_ge(sem("pool_in_ready"), 4)
            pe.wait_ge(sem("poolw_landed"), 16)
            pe.wait_ge(sem("xdt_ready"), 2)
            for t in range(2):
                o = mm(ps[:, 6, t * T:t * T + T], poolw[:, t, :], pools[:, t, :], start=True, stop=True)
            o.then_inc(sem("pool_ready"), 1)
            pe.wait_ge(sem("btok_copied"), 1)
            pe.wait_ge(sem("xw_ready"), 1)
            for g in range(2):
                o = mm(ps[:, 5, 192 * g:192 * g + 192], btok[:, g, :], xw[:, 192 * g:192 * g + 192],
                       start=True, stop=True)
            o.then_inc(sem("prev_ready"), 1)
            pe.wait_ge(sem("prev_copied"), 1)
            pe.wait_ge(sem("m_ready"), 4)
            pe.wait_ge(sem("ce_ready"), 2)
            for h in range(HEADS1):
                t, a = h // 2, 64 * (h % 2)
                w = slice(64 * h, 64 * h + 64)
                mm(ps[a:a + 64, t, 0:P], xdt[:, 0, w], seg[:, h, :], start=True, stop=True)
                mm(ps[a:a + 64, t, P:T], xdt[:, 1, w], seg[:, 6 + h, :], start=True, stop=False)
                o = mm(ps[a:a + 64, t, P:T], prev[:, w], CE[:, h, :], start=False, stop=True)
            o.then_inc(sem("y1_ready"), 1)
            pe.wait_ge(sem("ysq_ready"), 1)
            mm(ps[:, 3, 0:T], ones, ysq[:, 0, :], start=True, stop=False)
            mm(ps[:, 3, 0:T], ones[0:64, :], ysq[0:64, 1, :], start=False, stop=True)
            mm(ps[:, STAT, 0:T], ones, ysq[:, 2, :], start=True, stop=False)
            mm(ps[:, STAT, 0:T], ones[64:128, :], ysq[64:128, 1, :], start=False, stop=True)\
                .then_inc(sem("ystat_ready"), 1)

            pe.wait_ge(sem("mix_lo"), 1)
            stage("out1")
            pe.wait_ge(sem("yroot_ready"), 1)
            norm("ffn1")
            normed("ffn1")
            stage("up1", beside=lambda i, c: modulation((16 * i + 128, 8 * i + 56 + 2 * c), c))
            pe.wait_ge(sem("hl_done"), KH)
            stage("down1", hh1, hl1)
            pe.wait_ge(sem("lam_prod"), 1)
            mm(ps[:, 5, 0:2], ones[0:64, :], small[0:64, 80:82], start=True, stop=True)\
                .then_inc(sem("lam_dots"), 1)
            norm("final1")
            norm("pre2x")
            norm("pre2c")
            normed("pre2c")
            stage("up2")
            pe.wait_ge(sem("hl_done"), 2 * KH)
            stage("down2", hh2, hl2)
            for m in ("post2x", "post2c", "mod2x", "mod2c"):
                norm(m)
            normed("mod2c")
            for name in ("hy_x1", "hy_v", "hy_x0", "k2", "q2"):
                stage(name)
            stage("v2", token_major=True)
            stage("gate2")
            drained(pe, stages["gate2"])
            pe.wait_ge(sem("rot_done"), 16)

            def scores2(r):
                h, qt = r // 2, r % 2
                if r >= 2:
                    pe.wait_ge(sem("prob2_ready"), 2 * r - 2)
                for m in range(2):
                    a = 64 * m
                    o = mm(ps[:, 2 * (r % 2) + m, :], qT[a:a + 64, h, qt * P:qt * P + P],
                           kT[a:a + 64, h, :], start=True, stop=True)
                o.then_inc(sem("s2_ready"), 1)

            def turn2(r):
                pe.wait_ge(sem("pmix_ready"), r + 1)
                if r >= 2:
                    pe.wait_ge(sem("pt2_copied"), r - 1)
                for kt in range(4):
                    o = pe.transpose(ps[:, 4 + r % 2, kt * P:kt * P + P],
                                     p2[:, r % 2, 0, kt * P:kt * P + P], ident)
                o.then_inc(sem("pt2_ready"), 1)

            def values2(r):
                h = r // 2
                pe.wait_ge(sem("pt2_copied"), r + 1)
                if r >= 2:
                    pe.wait_ge(sem("otok_ready"), r - 1)
                for kt in range(4):
                    o = mm(ps[:, 6 + r % 2, 0:P], pT2[:, r % 2, kt, :], V[:, kt, h * P:h * P + P],
                           start=(kt == 0), stop=(kt == 3))
                o.then_inc(sem("o2_ready"), 1)

            scores2(0)
            for r in range(2 * HEADS2):
                if r + 1 < 2 * HEADS2:
                    scores2(r + 1)
                if r >= 1:
                    values2(r - 1)
                turn2(r)
            values2(2 * HEADS2 - 1)

            pe.wait_ge(sem("otok_ready"), 2 * HEADS2)
            pe.wait_ge(sem("z_landed"), 16)
            for l in range(3):
                w = pc(f"filt_w{l + 1}", 0, 64)
                if l:
                    pe.wait_ge(sem("sin_ready"), l)
                mm(ps[0:64, 6, 0:T], w[0:33, :] if l == 0 else w[0:64, :],
                   zT[0:33, :] if l == 0 else filt[:, 4, :], start=True, stop=True)\
                    .then_inc(sem("filt_pre"), 1)
            pe.wait_ge(sem("sin_ready"), 3)
            pe.wait_ge(sem("w4_landed"), 16)
            for g in range(8):
                lt, q = g // 4, g % 4
                if g >= 4:
                    pe.wait_ge(sem("hfb_ready"), g - 3)
                mm(ps[:, g % 4, :], filt[:, 4, lt * P:lt * P + P], w4[:, q * 512:q * 512 + 512],
                   start=True, stop=True).then_inc(sem("h_ready"), 1)
            pe.wait_ge(sem("abs_ready"), 1)
            for j in range(KD):
                for n in range(4):
                    o = mm(ps[:, 6, 256 + j:257 + j],
                           absk[:, n // 2, D * (n % 2) + j * P:D * (n % 2) + j * P + P],
                           ones[:, 0:1], start=(n == 0), stop=(n == 3))
            o.then_inc(sem("ksum_ready"), 1)
            pe.wait_ge(sem("u_ready"), KD)
            for g in range(4):
                tt, half = g // 2, g % 2
                for j in range(4):
                    o = pe.transpose(ps[:, g, j * P:j * P + P],
                                     u[:, 4 * half + j, tt * P:tt * P + P], ident)
                o.then_inc(sem("ut_ready"), 1)
            pe.wait_ge(sem("dft_landed"), 16)
            pe.wait_ge(sem("hsd_ready"), 2)
            for g in range(8):
                kind, ft, half = g // 4, g % 4 // 2, g % 2
                if g >= 4:
                    pe.wait_ge(sem("kf_copied"), g - 3)
                elif g == 2:
                    pe.wait_ge(sem("knorm_read"), 1)
                for tt in range(2):
                    o = mm(ps[:, 4 + g % 4, :], dft[:, 2 * kind + tt, ft * P:ft * P + P],
                           hsd[:, tt, D * kind + half * 512:D * kind + half * 512 + 512],
                           start=(tt == 0), stop=(tt == 1))
                o.then_inc(sem("kf_ready"), 1)
            pe.wait_ge(sem("ut_copied"), 4)
            for g in range(4):
                ft, half = g // 2, g % 2
                if g >= 2:
                    pe.wait_ge(sem("yf_ready"), g - 1)
                for kind in range(2):
                    for tt in range(2):
                        o = mm(ps[:, 2 * (g % 2) + kind, :], dft[:, 2 * kind + tt, ft * P:ft * P + P],
                               utok[:, tt, half * 512:half * 512 + 512], start=(tt == 0), stop=(tt == 1))
                o.then_inc(sem("uf_ready"), 1)
            pe.wait_ge(sem("yf_ready"), 4)
            for j in range(KD):
                if j >= 4:
                    pe.wait_ge(sem("yhy_ready"), j - 3)
                for n in range(4):
                    y = yre if n < 2 else yim
                    o = mm(ps[:, j % 4, 0:T], y[:, n % 2, j * P:j * P + P], dft[:, 4 + n, :],
                           start=(n == 0), stop=(n == 3))
                o.then_inc(sem("yc_ready"), 1)
            pe.wait_ge(sem("otok_scaled"), 1)
            pe.wait_ge(sem("kf_copied"), 8)
            for j in range(KD):
                if j >= 4:
                    pe.wait_ge(sem("o_lo"), j - 3)
                for qt in range(2):
                    o = pe.transpose(ps[:, 4 + j % 4, qt * P:qt * P + P], otok[:, 2 * j + qt, :], ident)
                o.then_inc(sem("ott_ready"), 1)
            pe.wait_ge(sem("o_lo"), KD)
            pe.wait_ge(sem("yhy_lo"), 1)
            stage("da_out")
            stage("hy_out", nh[:, :, T:2 * T], nl[:, :, T:2 * T])
            pe.wait_ge(sem("t_lo"), 1)
            stage("o2")
            norm("post_mix2")
            norm("pre3")
            normed("pre3")
            stage("up3")
            pe.wait_ge(sem("hl_done"), 3 * KH)
            stage("down3", hh1, hl1)
            norm("post3")


def pairs_before(name):
    return {"up1": 0, "up2": KH, "up3": 2 * KH}[name]


def slabs_of(w):
    k, n = w.shape
    return np.ascontiguousarray(w.reshape(k // P, P, n // P, P).transpose(2, 1, 0, 3)
                                .reshape(n // P, P, k))


def pair_slabs(w):
    s = slabs_of(w)
    n = s.shape[0] // 2
    return np.ascontiguousarray(np.stack([s[:n], s[n:]], axis=1).reshape(s.shape))


def half_slabs(w):
    s = slabs_of(w)
    return np.ascontiguousarray(s.reshape(KD, P, 2, KHH * P).transpose(0, 2, 1, 3)
                                .reshape(2 * KD, P, KHH * P))


def tiles(v):
    return v.reshape(-1, P).T


def kernel(**inputs):
    import concourse.bacc as bacc
    from concourse.bass_utils import run_bass_kernel_spmd

    g = {k: np.asarray(v) for k, v in inputs.items()}
    w_in = g["w_in"][0]
    n_dt = 6
    qkvzx, dt, pool = w_in[:, :2432], w_in[:, 2432:2438], w_in[:, 2438:]
    dt_pad = np.zeros((D, P), np.float32)
    dt_pad[:, :n_dt] = dt
    in1 = slabs_of(np.concatenate([qkvzx[:, 2048:], pool, dt_pad, qkvzx[:, :2048]], axis=1))

    params = np.zeros((P, NPAR), np.float32)

    def put(name, a, k=0):
        params[:a.shape[0], COL[name] + k:COL[name] + k + a.shape[1]] = a

    for name in ("norm_mix", "norm_ffn", "conv_w", "conv_b", "ssd_norm", "pool_scale"):
        put(name, tiles(g[name][0]))
    put("norm_final", tiles(g["norm_final"]))
    put("d_skip", tiles(np.repeat(g["d_skip"][0], 64)))
    put("b_ada", tiles(g["b_ada_2"][0]))
    put("norm_g", tiles(g["norm_g_2"][0]))
    put("hy_w", tiles(g["hy_conv_w_2"][0]))
    put("hy_b", tiles(g["hy_conv_b_2"][0]))
    put("hy_bias", tiles(g["hy_bias_2"][0]))
    for l in range(3):
        put("filt_b", g[f"filt_b{l + 1}_2"][0][:, None], l)
        put(f"filt_w{l + 1}", g[f"filt_w{l + 1}_2"][0])
    put("filt_freq", g["filt_freq_2"][0][:, None])
    put("subln", g["subln_g_2"][0][:, None])
    put("dt_bias", g["dt_bias"][0][:, None])
    put("a_log", g["a_log"][0][:, None])
    for n in (1, 2):
        put("lam_q", g[f"lambda_q{n}_2"][0][:, None], n - 1)
        put("lam_k", g[f"lambda_k{n}_2"][0][:, None], n - 1)
    pool_w = np.zeros((P, 2, P), np.float32)
    for n in range(4):
        a = 64 * (n % 2)
        pool_w[a:a + 64, n // 2, a:a + 64] = g["pool_w"][0, n]

    def tokens(a):
        return np.ascontiguousarray(a.T.reshape(KD, P, T).transpose(1, 0, 2))

    w_in2 = slabs_of(g["w_in_2"][0])
    arrays = dict(
        x=tokens(g["x"][0]), ctx=tokens(g["ctx_2"][0]), params=params, pool_w=pool_w,
        cvec=np.ascontiguousarray(np.stack([tiles(g["c_2"][0]), tiles(g["c_ctx_2"])], axis=2)),
        in1=in1, out1=slabs_of(g["w_out"][0]), up1=pair_slabs(g["w_gate_up"][0]),
        down1=half_slabs(g["w_down"][0]), w_ada=slabs_of(g["w_ada_2"][0]),
        up2=pair_slabs(g["w_ff_in_2"][0, 0]), down2=half_slabs(g["w_ff_out_2"][0, 0]),
        up3=pair_slabs(g["w_ff_in_2"][0, 1]), down3=half_slabs(g["w_ff_out_2"][0, 1]),
        in2=w_in2, hy_out=slabs_of(g["w_hy_out_2"][0]), da_out=slabs_of(g["w_da_out_2"][0]),
        o2=slabs_of(g["w_o_2"][0]), filt_w4=g["filt_w4_2"][0], **constants())

    nc = bacc.Bacc("TRN2", target_bir_lowering=False, num_devices=1)
    d = {n: nc.dram_tensor(f"in_{n}", a.shape, F32, kind="ExternalInput").ap() for n, a in arrays.items()}
    out = nc.dram_tensor("out_xT", (P, KD, T), F32, kind="ExternalOutput").ap()
    build(nc, d, out)
    r = run_bass_kernel_spmd(nc, [{f"in_{n}": a for n, a in arrays.items()}], core_ids=[0])
    y = r.results[0]["out_xT"]
    return y.transpose(2, 1, 0).reshape(1, T, D)
```

```python
from contextlib import ExitStack

import numpy as np

import concourse.bass as bass
from concourse import mybir

F32 = mybir.dt.float32
F32R = mybir.dt.float32r
ALU = mybir.AluOpType
ACT = mybir.ActivationFunctionType
AX = mybir.AxisListType

P = 128
D = 1024
KD = D // P
T = 256
FH = 2816
KH = FH // P
KHH = KH // 2
RAW = 4
HL = 2
BANKS = 4
EPS = 1e-6
NEG = -1e30
HEADS1 = 6
NT1 = 3
HEADS2 = 8
LAM_INIT = 0.2

Q1, K1, V1, Z1, XBC1, POOL1, DT1 = 0, 3, 6, 9, 12, 19, 21
N_IN1 = 22
HEAD_SLABS = 6

_WIDTHS = [("norm_mix", 8), ("norm_ffn", 8), ("norm_final", 8), ("conv_w", 28), ("conv_b", 7),
           ("d_skip", 3), ("ssd_norm", 3), ("pool_scale", 2), ("b_ada", 72), ("norm_g", 48),
           ("hy_w", 72), ("hy_b", 24), ("hy_bias", 8), ("filt_b", 3), ("filt_freq", 1),
           ("subln", 1), ("dt_bias", 1), ("a_log", 1), ("lam_q", 2), ("lam_k", 2),
           ("filt_w1", 64), ("filt_w2", 64), ("filt_w3", 64)]
COL, NPAR = {}, 0
for _n, _w in _WIDTHS:
    COL[_n] = NPAR
    NPAR += _w

CONSTS = [("ones", 128), ("ident", 128), ("tri", 128), ("mask384", 384), ("maskT", 128),
          ("eps", 1), ("one", 1), ("zero", 8)]
CC, NCON = {}, 0
for _n, _w in CONSTS:
    CC[_n] = NCON
    NCON += _w


def constants():
    a = np.arange(P)
    c = np.zeros((P, NCON), np.float32)
    c[:, CC["ones"]:CC["ones"] + 128] = 1.0
    c[:, CC["ident"]:CC["ident"] + 128] = np.eye(P)
    c[:, CC["tri"]:CC["tri"] + 128] = a[:, None] <= a[None, :]
    causal = np.where(a[None, :] <= a[:, None], 0.0, NEG)
    c[:, CC["mask384"]:CC["mask384"] + 128] = causal
    c[:, CC["mask384"] + 256:CC["mask384"] + 384] = causal
    c[:, CC["maskT"]:CC["maskT"] + 128] = causal.T
    c[:, CC["eps"]] = EPS
    c[:, CC["one"]] = 1.0
    t = np.arange(T)
    rcount = np.zeros((P, 2, T), np.float32)
    for g, w in enumerate((2, 4, 8, 16)):
        rcount[64 * (g % 2):64 * (g % 2) + 64, g // 2] = 1.0 / np.minimum(t + 1, w)
    p = np.arange(P)
    axis, half, i = p // 32 % 2, p // 16 % 2, p % 16
    inv = (np.float32(10000.0) ** (-(2 * i).astype(np.float32) / np.float32(32))).astype(np.float32)
    pos = np.where(axis[:, None] == 0, t[None, :] // 64, t[None, :] % 64).astype(np.float32)
    ang = (pos * inv[:, None]).astype(np.float32).astype(np.float64)
    rope = np.zeros((P, 2, T), np.float32)
    rope[:, 0] = np.cos(ang)
    rope[:, 1] = np.where(half[:, None] == 0, -np.sin(ang), np.sin(ang))
    th = np.pi * (2 * t[None, :] + 1) * t[:, None] / 512.0
    dft = np.zeros((P, 8, T), np.float32)
    dft[:, 0:2] = np.cos(th).reshape(2, P, T).transpose(1, 0, 2)
    dft[:, 2:4] = np.sin(th).reshape(2, P, T).transpose(1, 0, 2)
    dft[:, 4:6] = (np.cos(th).T / 256).reshape(2, P, T).transpose(1, 0, 2)
    dft[:, 6:8] = (np.sin(th).T / 256).reshape(2, P, T).transpose(1, 0, 2)
    bands = 16
    tl = np.linspace(0.0, 1.0, T, dtype=np.float32)[:, None]
    w = (2.0 * np.pi * t.astype(np.float32)[:, None] / T).astype(np.float32)
    f = np.linspace(1e-4, bands - 1, bands, dtype=np.float32)[None, :]
    z = np.concatenate([tl, np.cos(f * w), -np.sin(f * w)], axis=-1).astype(np.float32)
    zt = np.zeros((64, T), np.float32)
    zt[:33] = z.T
    deltas = np.linspace(np.log(1e-2) / 1.5, np.log(1e-2) / 0.3, D, dtype=np.float32)
    decay = np.exp(-tl * np.abs(deltas)[None]).astype(np.float32).reshape(2, P, D).transpose(1, 0, 2)
    return dict(consts=c, rcount=rcount, rope=rope, dft=dft, filt_z=zt, decay=np.ascontiguousarray(decay))


IN2 = {"hy_x0": 0, "hy_x1": 8, "hy_v": 16, "q2": 24, "k2": 32, "v2": 40, "gate_hy": 48, "gate_da": 56}


ADA_RIDES = {"in1_head": 4, "in1": 6, "out1": 16, "up1": 20, "down1": 34, "up2": 42, "down2": 64}
ADA_TRIPS = {"up1": 7}
ADA_START, ADA_MIXERS, N_ADA_BOTH, N_ADA = 4, 14, 42, 72


class Stage:

    def __init__(self, name, slabs, kt=KD, per_out=1, cols=T, body=4, first=None, banks=BANKS):
        self.name, self.slabs, self.kt, self.per_out = name, slabs, kt, per_out
        self.weights = "in2" if name in IN2 else name.replace("_head", "")
        self.cols, self.body, self.banks = cols, body, banks
        self.first = IN2.get(name, 0) if first is None else first
        self.trips = slabs // body
        assert self.trips * body == slabs


def plan():
    st = [Stage("in1_head", HEAD_SLABS, body=HEAD_SLABS),
          Stage("in1", N_IN1 - HEAD_SLABS, first=HEAD_SLABS),
          Stage("out1", KD), Stage("up1", 2 * KH), Stage("down1", 2 * KD, kt=KHH, per_out=2),
          Stage("up2", 2 * KH, cols=2 * T), Stage("down2", 2 * KD, kt=KHH, per_out=2, cols=2 * T),
          Stage("k2", 8, cols=2 * T), Stage("v2", 8, cols=2 * T), Stage("q2", 8),
          Stage("hy_x1", 8, banks=2), Stage("hy_v", 8, banks=2), Stage("hy_x0", 8, banks=2),
          Stage("gate_hy", 8, banks=2), Stage("gate_da", 8, banks=2),
          Stage("hy_out", 8), Stage("da_out", 8), Stage("o2", 8),
          Stage("up3", 2 * KH), Stage("down3", 2 * KD, kt=KHH, per_out=2)]
    s = 0
    uses = [0] * BANKS
    for n, x in enumerate(st):
        x.s0, x.uses0 = s, list(uses)
        x.next = st[n + 1] if n + 1 < len(st) else None
        s += x.slabs
        for k in range(x.body // x.per_out):
            uses[k % x.banks] += x.trips
        x.uses1, x.s1 = list(uses), s
    return {x.name: x for x in st}, st


WOVEN = ("hy_x1", "hy_v", "hy_x0", "gate_hy", "gate_da", "hy_out")


def woven(stages):
    return [(8 * n + 4 * i + c, stages[name], i, c)
            for n, name in enumerate(WOVEN) for i in range(2) for c in range(4)]


NORMS = ["mix1", "ffn1", "pre2c", "final1", "pre2x", "post2x", "post2c", "mod2x", "mod2c",
         "post_mix2", "pre3", "post3"]


def build(nc, d, out):
    stages, order = plan()
    with ExitStack() as ctx:
        def keep(name, shape, dt=F32):
            return ctx.enter_context(nc.sbuf_tensor(name, shape, dt))

        def place(at, name, shape, dt=F32):
            with ExitStack() as held:
                if at:
                    held.enter_context(nc.sbuf_tensor(f"below_{name}", [P, at // 4], F32))
                return held.enter_context(nc.sbuf_tensor(name, shape, dt))

        names = {}

        def sem(name):
            if name not in names:
                names[name] = ctx.enter_context(nc.semaphore(name))
            return names[name]

        KB = 1024
        xT = keep("xT", [P, KD, 2 * T])
        con = keep("con", [P, NCON])
        par = keep("par", [P, NPAR])
        mod = keep("mod", [P, 9 * KD, 2])
        gmod = keep("gmod", [P, 9, KD])
        small = keep("small", [P, 256])
        idle = keep("idle", [P, 16])
        rinv = keep("rinv", [P, T])
        rtmp = keep("rtmp", [P, T])
        raw = keep("raw", [P, RAW, KHH * P])
        hi = keep("hi", [P, HL, KHH * P], F32R)
        lo = keep("lo", [P, HL, KHH * P], F32R)
        act_c = place(0, "act_c", [P, KD, 2 * T])
        nl = keep("nl", [P, KD, 2 * T], F32R)
        proj = place(0, "proj", [P, KD, 2 * T])
        nh = keep("nh", [P, KD, 2 * T], F32R)

        sq = place(0, "sq", [P, KD, T])
        xg = place(8 * KB, "xg", [P, KD, T])
        u1 = place(0, "u1", [P, N_IN1, T])
        cT = place(22 * KB, "cT", [P, 7, T])
        mixT = place(29 * KB, "mixT", [P, KD, T])
        vtok = place(37 * KB, "vtok", [P, 2, 384])
        scor = place(40 * KB, "scor", [P, 2, 384])
        prob = place(43 * KB, "prob", [P, 2, 384])
        pT = place(46 * KB, "pT", [P, 2, 384])
        rcount = place(49 * KB, "rcount_s", [P, 2, T])
        poolw = place(51 * KB, "poolw", [P, 2, P])
        seg = place(52 * KB, "seg", [P, 12, P])
        triA = place(58 * KB, "triA", [P, 12, P])
        CE = place(64 * KB, "CE", [P, 6, P])
        xdt = place(67 * KB, "xdt", [P, 2, 384])
        xw = place(70 * KB, "xw", [P, 384])
        prev = place(71 * KB + 512, "prev", [P, 384])
        btok = place(73 * KB, "btok", [P, 2, P])
        dtA = place(74 * KB, "dtA", [8, 4, T])
        pools = place(78 * KB, "pools", [P, 6, T])
        yssd = place(84 * KB, "yssd", [P, 3, T])
        ysq = place(87 * KB, "ysq", [P, 3, T])
        yroot = place(58 * KB, "yroot", [P, 2, T])
        yrg = place(60 * KB, "yrg", [P, 2, T])
        ada = place(96 * KB, "ada", [P, 2, KD * P])
        hh1 = place(0, "hh1", [P, KH, T], F32R)
        hl1 = place(22 * KB, "hl1", [P, KH, T], F32R)
        sg1 = place(44 * KB, "sg1", [P, 2, T])
        pr1 = place(46 * KB, "pr1", [P, 2, T])
        hh2 = place(0, "hh2", [P, KH, 2 * T], F32R)
        hl2 = place(44 * KB, "hl2", [P, KH, 2 * T], F32R)
        sg2 = place(88 * KB, "sg2", [P, 2, 2 * T])
        pr2 = place(92 * KB, "pr2", [P, 2, 2 * T])
        filt = place(56 * KB, "filt", [64, 4, T])
        zT = place(60 * KB, "zT", [64, T])
        filt3 = place(104 * KB, "filt3", [64, T])
        w4 = place(16 * KB, "w4_s", [64, 2 * D])
        decay = place(24 * KB, "decay_s", [P, 2, D])
        hfb = place(42 * KB, "hfb", [P, 2, 2 * D])
        hsd = place(58 * KB, "hsd", [P, 2, 2 * D])
        absk = place(74 * KB, "absk", [P, 2, 2 * D])
        kre = place(16 * KB, "kre", [P, 2, D])
        kim = place(24 * KB, "kim", [P, 2, D])
        u = place(0, "u", [P, KD, T])
        x0 = place(8 * KB, "x0", [P, KD, T])
        gT = place(16 * KB, "gT", [P, 2 * KD, T])
        rope = place(32 * KB, "rope_s", [P, 2, T])
        dft = place(34 * KB, "dft_s", [P, 8, T])
        otok = place(42 * KB, "otok", [P, 2 * HEADS2, P])
        qT = place(50 * KB, "qT", [P, KD, T])
        kT = place(58 * KB, "kT", [P, KD, 2 * T])
        V = place(74 * KB, "V", [P, 4, D])
        cvt = place(90 * KB, "cvt", [P, 4, T])
        rot = place(94 * KB, "rot", [P, 2, 2, T])
        p2 = place(94 * KB, "p2", [P, 2, 2, 2 * T])
        pT2 = place(102 * KB, "pT2", [P, 2, 4, P])
        yt = place(90 * KB, "yt", [P, 4, T])

        def halves(x, n, half):
            r = 4 * n + 2 * half
            return x[:, r:r + 2, T:2 * T]

        tT = place(50 * KB, "tT", [P, KD, T])
        tda = place(58 * KB, "tda", [P, 4, T])

        ps = ctx.enter_context(nc.psum_tensor("ps", [P, 8, 512], F32))

        def cc(name, n=1):
            return con[:, CC[name]:CC[name] + n]

        def pc(name, k=0, n=1):
            return par[:, COL[name] + k:COL[name] + k + n]

        ones, ident, tri = cc("ones", P), cc("ident", P), cc("tri", P)
        STAT = 4
        raw_landed = [sem(f"raw_landed{r}") for r in range(RAW)]
        hi_done, lo_done, slab_used = sem("hi_done"), sem("lo_done"), sem("slab_used")
        bank_free = [sem(f"bank_free{b}") for b in range(BANKS)]
        block = ctx.enter_context(nc.Block())

        def slab(st, i, c):
            return st.s0 + st.body * i + c

        def uses(st, i, oc):
            b = oc % st.banks
            per_trip = len([k for k in range(st.body // st.per_out) if k % st.banks == b])
            return st.uses0[b] + per_trip * i + oc // st.banks

        def ahead(st, i, c):
            if c + HL < st.body:
                return st, i, c + HL
            if isinstance(i, int) and i == st.trips - 1:
                return (st.next, 0, c + HL - st.body) if st.next else None
            return st, i + 1, c + HL - st.body

        def trips(eng, st, body):
            if st.trips == 2:
                body(0)
            elif st.trips > 2:
                with eng.Fori(0, st.trips - 1) as i:
                    body(i)
            body(st.trips - 1)

        def wait(eng, s, n):
            if not (isinstance(n, int) and n <= 0):
                eng.wait_ge(s, n)

        def drained(eng, st):
            for b in range(BANKS):
                wait(eng, bank_free[b], st.uses1[b])

        SPLIT = [m for m in NORMS if m[:3] in ("mix", "ffn", "pre", "mod")]
        UPDATE = [m for m in NORMS if m not in SPLIT]

        def norm_of(m):
            x, c = slice(0, T), slice(T, 2 * T)
            src, cols = xT, (c if m[-2:] == "2c" else x)
            if m[:4] == "post":
                src = proj
            gain = {"mix1": lambda k: pc("norm_mix", k), "ffn1": lambda k: pc("norm_ffn", k),
                    "final1": lambda k: pc("norm_final", k)}.get(m)
            if gain is None:
                row = ["pre2x", "pre2c", "post2x", "post2c", "mod2x", "mod2c", "post_mix2", "pre3",
                       "post3"].index(m)
                gain = lambda k: gmod[:, row, k:k + 1]
            q = {"pre2": 0, "mod2": 3, "pre3": 6}.get(m[:4])
            if q is None:
                shift = lambda k: cc("zero")
            else:
                shift = lambda k: mod[:, 8 * q + k, (1 if m[-1] == "c" else 0):(2 if m[-1] == "c" else 1)]
            return src, cols, gain, shift

        @block.sync
        def _(sp):
            sp.dma_start(xT[:, :, 0:T], d["x"]).then_inc(sem("x_landed"), 16)
            sp.dma_start(con[:, :], d["consts"]).then_inc(sem("con_landed"), 16)
            sp.dma_start(par[:, :], d["params"]).then_inc(sem("par_landed"), 16)

            def load(st, i, c):
                r = (st.s0 + c) % RAW
                wait(sp, lo_done, slab(st, i, c) - RAW + 1)
                sp.dma_start(raw[:, r, 0:st.kt * P], d[st.weights][st.first + st.body * i + c])\
                  .then_inc(raw_landed[r], 16)

            def load_ada(n, r):
                wait(sp, sem("ada_used"), n - 1)
                sp.dma_start(ada[:, r, :], d["w_ada"][n]).then_inc(sem(f"ada_landed{r}"), 16)

            def load_trip(st, i, rides=True):
                for c in range(st.body):
                    load(st, i, c)
                    if rides and st.name in ADA_RIDES and c in (1, 3):
                        load_ada(ADA_RIDES[st.name] + 2 * i + c // 2, c // 2)

            for st in order:
                if st.name == "in1_head":
                    for n in range(2):
                        load_ada(n, n % 2)
                if st.name == "out1":
                    for c in range(st.body):
                        load(st, 0, c)
                    for n in range(ADA_MIXERS, ADA_RIDES["out1"] + 2):
                        load_ada(n, n % 2)
                    load_trip(st, 1)
                    continue
                if st.name == "in1_head":
                    for c in range(4):
                        load(st, 0, c)
                    for n in (2, 3, 4, 5):
                        load_ada(n, n % 2)
                    for c in (4, 5):
                        load(st, 0, c)
                    continue
                if st.name == "k2":
                    load_trip(st, 0)
                    sp.wait_ge(slab_used, stages["down2"].s1)
                    sp.dma_start(w4[:, :], d["filt_w4"]).then_inc(sem("w4_landed"), 16)
                    sp.dma_start(decay[:, :, :], d["decay"]).then_inc(sem("decay_landed"), 16)
                    sp.dma_start(dft[:, :, :], d["dft"]).then_inc(sem("dft_landed"), 16)
                    sp.dma_start(rope[:, :, :], d["rope"]).then_inc(sem("rope_landed"), 16)
                    load_trip(st, 1)
                    continue
                if st.trips == 1:
                    load_trip(st, 0)
                else:
                    cut = ADA_TRIPS.get(st.name, st.trips)
                    with sp.Fori(0, cut) as i:
                        load_trip(st, i)
                    if cut < st.trips:
                        with sp.Fori(cut, st.trips) as i:
                            load_trip(st, i, rides=False)
            sp.wait_ge(sem("x_updated"), 8 * len(UPDATE))
            sp.dma_start(out, xT[:, :, 0:T]).then_inc(sem("out_landed"), 16)
            sp.wait_ge(sem("out_landed"), 16)

        @block.gpsimd
        def _(pool):
            for b in range(BANKS):
                pool.wait_ge(bank_free[b], stages["in1"].uses1[b])
            pool.wait_ge(sem("rcount_landed"), 16)
            n = 0

            def step(ins):
                nonlocal n
                n += 1
                ins.then_inc(sem("pool_step"), 1)
                pool.wait_ge(sem("pool_step"), n)

            sums = [u1[:, POOL1:POOL1 + 2, :], pools[:, 0:2, :], pools[:, 2:4, :],
                    pools[:, 4:5, :], pools[:, 5:6, :]]
            for lvl in range(4):
                w, a, to = 1 << lvl, sums[lvl], sums[lvl + 1]
                if lvl == 2:
                    a = a[:, 1:2, :]
                step(pool.tensor_tensor(to[:, :, w:T], a[:, :, w:T], a[:, :, 0:T - w], ALU.add))
                step(pool.tensor_copy(to[:, :, 0:w], a[:, :, 0:w]))
            for g, s in enumerate((pools[0:64, 0, :], pools[64:128, 2, :], pools[0:64, 4, :],
                                   pools[64:128, 5, :])):
                h0, tl = 64 * (g % 2), g // 2
                step(pool.tensor_tensor(s, s, rcount[h0:h0 + 64, tl, :], ALU.mult))
                pool.tensor_tensor(pools[h0:h0 + 64, tl, :], s, u1[h0:h0 + 64, POOL1 + tl, :],
                                   ALU.subtract).then_inc(sem("pool_in_ready"), 1)
            pool.wait_ge(sem("abs_ready"), 1)
            step(pool.tensor_tensor(absk[:, 0, :], absk[:, 0, :], absk[:, 1, :], ALU.add))
            pool.tensor_tensor(absk[:, 0, 0:D], absk[:, 0, 0:D], absk[:, 0, D:2 * D], ALU.add)\
                .then_inc(sem("abs_summed"), 1)
            for i in range(2):
                for c in range(4):
                    st, j = stages["hy_v"], 4 * i + c
                    pool.wait_ge(bank_free[c % 2], uses(st, i, c) + 1)
                    pool.tensor_tensor(u[:, j, :], u[:, j, :], cvt[:, c, :], ALU.mult)\
                        .then_inc(sem("u_ready"), 1)

        @block.scalar
        def _(act):
            act.dma_start(act_c[:, :, T:2 * T], d["cvec"]).then_inc(sem("c_landed"), 16)
            act.dma_start(zT[:, :], d["filt_z"]).then_inc(sem("z_landed"), 16)
            act.dma_start(rcount[:, :, :], d["rcount"]).then_inc(sem("rcount_landed"), 16)
            act.dma_start(poolw[:, :, :], d["pool_w"]).then_inc(sem("poolw_landed"), 16)
            act.dma_start(xT[:, :, T:2 * T], d["ctx"]).then_inc(sem("ctx_landed"), 16)

            def split(st, i, c):
                s, r, h, n = slab(st, i, c), (st.s0 + c) % RAW, (st.s0 + c) % HL, st.kt * P
                lap = (st.s0 + c) // RAW + (i if st.body == RAW else 0)
                act.wait_ge(raw_landed[r], 16 * lap + 16)
                wait(act, slab_used, s - HL + 1)
                act.activation(hi[:, h, 0:n], raw[:, r, 0:n], ACT.Copy).then_inc(hi_done, 1)

            def epilogue(st, i, c):
                oc, col, kind = c // st.per_out, st.body * i + c, st.name
                if (c + 1) % st.per_out:
                    return
                b = oc % st.banks
                got = ps[:, b, 0:st.cols]
                n_used = slab(st, i, c) + 1
                if kind == "in1_head" or kind == "in1":
                    act.wait_ge(slab_used, n_used)
                    to = u1[:, 16 + c, :] if kind == "in1_head" else u1[:, col, :]
                    act.activation(to, got, ACT.Copy).then_inc(bank_free[b], 1)
                elif kind[:2] == "up":
                    q = c // 2
                    sg, pr, hh = (sg2, pr2, hh2) if st.cols > T else (sg1, pr1, hh1)
                    if c % 2 == 0:
                        act.wait_ge(slab_used, n_used)
                        act.activation(sg[:, q, :], got, ACT.Silu).then_inc(bank_free[b], 1)
                    else:
                        act.wait_ge(bank_free[b], uses(st, i, oc) + 1)
                        act.activation(hh[:, 2 * i + q, :], pr[:, q, :], ACT.Copy)\
                           .then_inc(sem("hh_done"), 1)
                elif kind in ("down2", "down3", "o2"):
                    act.wait_ge(slab_used, n_used)
                    j = (st.body // st.per_out) * i + oc
                    act.activation(proj[:, j, 0:st.cols], got, ACT.Copy).then_inc(bank_free[b], 1)
                elif kind[:3] == "hy_" and kind != "hy_out":
                    act.wait_ge(slab_used, n_used)
                    to = cvt[:, c, :] if kind == "hy_v" else (u if kind == "hy_x1" else x0)[:, col, :]
                    if kind == "hy_v" and i:
                        act.wait_ge(sem("u_ready"), col - 3)
                    j = st.first + col
                    act.activation(to, got, ACT.Identity,
                                   scale=par[:, bass.ds(COL["hy_w"] + 24 + j, 1)],
                                   bias=par[:, bass.ds(COL["hy_b"] + j, 1)])\
                       .then_inc(sem("conv_mid"), 1)
                elif kind == "k2":
                    act.wait_ge(slab_used, n_used)
                    act.activation(kT[:, col, T:2 * T], ps[:, b, T:2 * T], ACT.Copy)\
                       .then_inc(sem("k_ctx_done"), 1)
                elif kind == "v2":
                    if c == st.body - 1:
                        act.wait_ge(slab_used, n_used)
                        for tt in range(4):
                            act.activation(V[:, tt, bass.ds(512 * i, 512)], ps[:, tt, :], ACT.Copy)\
                               .then_inc(bank_free[tt], 1)
                elif kind[:4] == "gate":
                    act.wait_ge(slab_used, n_used)
                    act.wait_ge(sem("yf_ready"), 4)
                    act.activation(gT[:, st.first - IN2["gate_hy"] + col, :], got, ACT.Copy)\
                       .then_inc(bank_free[b], 1)

            def stage(name):
                st = stages[name]

                def body(i):
                    for c in range(st.body):
                        nxt = ahead(st, i, c)
                        if nxt:
                            split(*nxt)
                        epilogue(st, i, c)

                if name[:2] == "up":
                    act.activation(idle[:, 0:1], cc("zero"), ACT.Silu).then_inc(sem("primed"), 1)
                trips(act, st, body)

            def squares(m, of=None):
                src, cols, _, _ = norm_of(m)
                for k in range(KD):
                    if of:
                        act.wait_ge(sem("x_updated"), 8 * UPDATE.index(of) + k + 1)
                    act.activation(sq[:, k, :], src[:, k, cols], ACT.Square).then_inc(sem("sq_ready"), 1)

            def root(m):
                n = NORMS.index(m)
                act.activation(idle[:, 4 + n:5 + n], cc("one"), ACT.Sqrt).then_inc(sem("primed"), 1)
                act.wait_ge(sem("stat_ready"), n + 1)
                wait(act, sem("rinv_ready"), n)
                act.activation(rtmp[:, :], ps[:, STAT, 0:T], ACT.Sqrt, scale=1.0 / D,
                               bias=cc("eps")).then_inc(sem("root_ready"), 1)

            def rounded(m):
                _, cols, _, shift = norm_of(m)
                for k in range(KD):
                    act.wait_ge(sem("xg_ready"), 8 * SPLIT.index(m) + k + 1)
                    act.activation(nh[:, k, cols], xg[:, k, :], ACT.Identity, bias=shift(k))\
                       .then_inc(sem("nh_ready"), 1)

            def norm(m, of=None):
                squares(m, of)
                root(m)
                if m in SPLIT:
                    rounded(m)

            act.wait_ge(sem("c_landed"), 16)
            act.activation(act_c[:, :, T:2 * T], act_c[:, :, T:2 * T], ACT.Silu)\
               .then_inc(sem("c_ready"), 1)
            for n in range(3):
                act.wait_ge(sem("sin_arg"), n + 1)
                act.activation(filt3[:, :], filt[:, 3, :], ACT.Sin).then_inc(sem("sin_ready"), 1)
            split(order[0], 0, 0)
            split(order[0], 0, 1)
            act.wait_ge(sem("x_landed"), 16)
            act.wait_ge(sem("con_landed"), 16)
            act.wait_ge(sem("par_landed"), 16)
            norm("mix1")
            stage("in1_head")
            stage("in1")

            act.activation(small[0:6, 0:1], pc("a_log")[0:6, :], ACT.Exp).then_inc(sem("a_ready"), 1)
            act.wait_ge(sem("dt_biased"), 1)
            act.activation(dtA[0:6, 3, :], dtA[0:6, 2, :], ACT.Abs).then_inc(sem("dt_step"), 1)
            act.wait_ge(sem("dt_step"), 1)
            act.activation(dtA[0:6, 3, :], dtA[0:6, 3, :], ACT.Exp, scale=-1.0).then_inc(sem("dt_step"), 1)
            act.wait_ge(sem("dt_step"), 2)
            act.activation(dtA[0:6, 3, :], dtA[0:6, 3, :], ACT.Ln, bias=cc("one")[0:6, :])\
               .then_inc(sem("dt_step"), 1)
            act.wait_ge(sem("vt_ready"), 1)
            act.activation(vtok[:, :, :], ps[:, 5:7, 0:384], ACT.Copy).then_inc(sem("vtok_copied"), 1)

            def out_pair(t):
                act.wait_ge(sem("o1_ready"), 2 * t + 2)
                act.activation(mixT[:, t, :], ps[:, 5 + t % 2, 0:T], ACT.Copy)\
                   .then_inc(sem("o1_copied"), 1)

            for h in range(HEADS1):
                r = h % 2
                act.wait_ge(sem("nmax_ready"), 2 * h + 2)
                if h >= 2:
                    act.wait_ge(sem("pt_ready"), h - 1)
                for qt, (a, b) in enumerate(((0, 128), (128, 384))):
                    act.activation(prob[:, r, a:b], scor[:, r, a:b], ACT.Exp,
                                   bias=small[:, 2 + 2 * h + qt:3 + 2 * h + qt],
                                   accum_out=small[:, 14 + 2 * h + qt:15 + 2 * h + qt])\
                       .then_inc(sem("prob_ready"), 1)
                act.wait_ge(sem("pt_ready"), h + 1)
                act.activation(pT[:, r, :], ps[:, 2 + r, 0:384], ACT.Copy).then_inc(sem("pt_copied"), 1)
                if h in (2, 4):
                    out_pair(h // 2 - 1)
            out_pair(2)

            act.wait_ge(sem("conv1_done"), 7)
            act.activation(cT[:, :, :], cT[:, :, :], ACT.Silu).then_inc(sem("cT_ready"), 1)
            act.activation(u1[:, Z1:Z1 + 3, :], u1[:, Z1:Z1 + 3, :], ACT.Silu).then_inc(sem("z_ready"), 1)
            act.wait_ge(sem("bt_ready"), 1)
            act.activation(btok[:, :, :], ps[:, STAT, 64:320].rearrange("p (g n) -> p g n", g=2),
                           ACT.Copy).then_inc(sem("btok_copied"), 1)
            act.wait_ge(sem("dte_arg"), 1)
            act.activation(small[:, 64:70], small[:, 64:70], ACT.Exp).then_inc(sem("dte_ready"), 1)
            act.wait_ge(sem("arow_ready"), 1)
            act.activation(CE[:, 0:2, :], ps[:, 1, 256:512].rearrange("p (a n) -> p a n", a=2),
                           ACT.Exp).then_inc(sem("ce_exp"), 1)
            act.activation(CE[:, 2:6, :], ps[:, 2, :].rearrange("p (a n) -> p a n", a=4),
                           ACT.Exp).then_inc(sem("ce_exp"), 1)
            act.wait_ge(sem("seg_ready"), 12)
            act.activation(seg[:, :, :], seg[:, :, :], ACT.Exp).then_inc(sem("decay1_ready"), 1)
            act.wait_ge(sem("prev_ready"), 1)
            act.activation(prev[:, :], ps[:, 5, 0:384], ACT.Copy).then_inc(sem("prev_copied"), 1)
            for t in range(2):
                act.wait_ge(sem("pool_ready"), 1)
                act.activation(mixT[:, 6 + t, :], ps[:, 6, t * T:t * T + T], ACT.Copy,
                               scale=pc("pool_scale", t)).then_inc(sem("pool_copied"), 1)
            act.wait_ge(sem("gated_ready"), 1)
            act.activation(ysq[:, :, :], yssd[:, :, :], ACT.Square).then_inc(sem("ysq_ready"), 1)
            act.activation(idle[:, 3:4], cc("one"), ACT.Sqrt).then_inc(sem("primed"), 1)
            act.wait_ge(sem("ystat_ready"), 1)
            act.activation(yroot[:, :, :], ps[:, 3:5, 0:T], ACT.Sqrt, scale=1.0 / 192, bias=cc("eps"))\
               .then_inc(sem("yroot_ready"), 1)
            act.wait_ge(sem("o1_copied"), 3)
            act.wait_ge(sem("pool_copied"), 2)
            act.activation(nh[:, 0:3, 0:T], mixT[:, 0:3, :], ACT.Copy).then_inc(sem("mix_hi"), 1)
            act.activation(nh[:, 6:8, 0:T], mixT[:, 6:8, :], ACT.Copy).then_inc(sem("mix_hi"), 1)
            act.wait_ge(sem("mix_ready"), 1)
            act.activation(nh[:, 3:6, 0:T], mixT[:, 3:6, :], ACT.Copy).then_inc(sem("mix_hi"), 1)

            stage("out1")
            drained(act, stages["out1"])
            norm("ffn1")
            stage("up1")
            stage("down1")
            act.wait_ge(slab_used, stages["down1"].s1)
            act.activation(ps[:, 6:8, :].rearrange("p b (k n) -> p (b k) n", k=2), act_c[:, 0:4, T:2 * T],
                           ACT.Copy).then_inc(sem("c_moved"), 1)
            act.wait_ge(sem("ctx_landed"), 16)
            squares("pre2c")
            root("pre2c")
            drained(act, stages["down1"])
            squares("final1")
            rounded("pre2c")
            root("final1")
            norm("pre2x", of="final1")
            act.wait_ge(sem("lam_dots"), 1)
            act.activation(small[:, 82:84], ps[:, 5, 0:2], ACT.Exp).then_inc(sem("lam_exp"), 1)
            stage("up2")
            stage("down2")
            drained(act, stages["down2"])
            norm("post2x")
            norm("post2c")
            squares("mod2x", of="post2x")
            root("mod2x")
            squares("mod2c", of="post2c")
            rounded("mod2x")

            def spectra(g0, g1):
                for g in range(g0, g1):
                    to = kre if g < 4 else kim
                    ft, half = g % 4 // 2, g % 2
                    act.wait_ge(sem("kf_ready"), g + 1)
                    act.activation(to[:, ft, half * 512:half * 512 + 512], ps[:, g % 4, :], ACT.Copy)\
                       .then_inc(sem("kf_copied"), 1)

            spectra(0, 4)
            root("mod2c")
            rounded("mod2c")
            spectra(4, 8)
            act.wait_ge(sem("hfb_ready"), 8)
            act.activation(absk[:, :, :], hfb[:, :, :], ACT.Abs).then_inc(sem("abs_ready"), 1)
            for name in ("k2", "v2", "q2"):
                stage(name)

            def exponentials(r):
                act.wait_ge(sem("nmax2_ready"), r + 1)
                if r >= 2:
                    act.wait_ge(sem("pt2_ready"), r - 1)
                for m in range(2):
                    act.activation(p2[:, r % 2, m, :], ps[:, 4 + m, :], ACT.Exp,
                                   scale=0.125, bias=small[:, 96 + 2 * r + m:97 + 2 * r + m],
                                   accum_out=small[:, 128 + 2 * r + m:129 + 2 * r + m])\
                       .then_inc(sem("prob2_ready"), 1)

            def move_head(r):
                act.wait_ge(sem("pt2_ready"), r + 1)
                act.activation(pT2[:, r % 2, :, :], ps[:, 6, :].rearrange("p (k q) -> p k q", k=4),
                               ACT.Copy).then_inc(sem("pt2_copied"), 1)

            def take_out(r):
                act.wait_ge(sem("o2_ready"), r + 1)
                act.activation(otok[:, r, :], ps[:, 7, 0:P], ACT.Copy,
                               scale=small[:, 160 + 2 * r:161 + 2 * r]).then_inc(sem("otok_ready"), 1)

            for p, st, i, c in woven(stages):
                if p < 32 and p % 2 == 0:
                    exponentials(p // 2)
                split(*ahead(st, i, c))
                epilogue(st, i, c)
                if 2 <= p <= 32 and p % 2 == 0:
                    take_out(p // 2 - 1)
                elif p < 32 and p % 2:
                    move_head(p // 2)
                if 16 <= p < 20:
                    g = p - 16
                    act.wait_ge(sem("ut_ready"), g + 1)
                    act.activation(halves(xT, g // 2, g % 2),
                                   ps[:, 2 + g % 2, :].rearrange("p (a n) -> p a n", a=2), ACT.Copy)\
                       .then_inc(sem("ut_copied"), 1)
                if p == 34:
                    act.wait_ge(sem("oss_ready"), 2 * HEADS2)
                    act.activation(small[:, 208:224], small[:, 192:208], ACT.Sqrt, scale=1.0 / P,
                                   bias=cc("eps")).then_inc(sem("oroot_ready"), 1)
                if p == 35:
                    act.wait_ge(sem("yhy_ready"), KD)
                    act.activation(nh[:, :, T:2 * T], x0[:, :, :], ACT.Copy).then_inc(sem("yhy_hi"), 1)
                if p in (36, 39):
                    drained(act, stages["gate_hy" if p == 36 else "gate_da"])
                    o = 0 if p == 36 else KD
                    act.activation(gT[:, o:o + KD, :], gT[:, o:o + KD, :], ACT.Sigmoid)\
                       .then_inc(sem("gates_ready"), 1)
                if p >= 40:
                    j = p - 40
                    act.wait_ge(sem("ott_ready"), j + 1)
                    act.activation(nh[:, j, 0:T], ps[:, 4 + j % 4, 0:T], ACT.Copy, scale=small[:, 84:85])\
                       .then_inc(sem("o_hi"), 1)
            st = stages["da_out"]
            for i in range(2):
                for c in range(4):
                    split(*ahead(st, i, c))
                    act.wait_ge(sem("tT_ready"), 4 * i + c + 1)
                    act.activation(nh[:, 4 * i + c, T:2 * T], tT[:, 4 * i + c, :], ACT.Copy)\
                       .then_inc(sem("t_hi"), 1)
            stage("o2")
            drained(act, stages["o2"])
            norm("post_mix2")
            norm("pre3", of="post_mix2")
            stage("up3")
            stage("down3")
            drained(act, stages["down3"])
            norm("post3")

        @block.vector
        def _(dve):
            n = 0

            def step(ins):
                nonlocal n
                n += 1
                ins.then_inc(sem("dve_step"), 1)
                return n

            def after(k):
                dve.wait_ge(sem("dve_step"), k)

            def split(st, i, c):
                s, r, h, w = slab(st, i, c), (st.s0 + c) % RAW, (st.s0 + c) % HL, st.kt * P
                dve.wait_ge(hi_done, s + 1)
                dve.tensor_tensor(lo[:, h, 0:w], raw[:, r, 0:w], hi[:, h, 0:w].bitcast(F32),
                                  ALU.subtract).then_inc(lo_done, 1)

            def short_taps(c, col, st, b, to):
                k = (stages["hy_x1"].s0, )[0]
                done = slab(st, 0, 0) - k + st.body * (col[0]) + c + 1
                dve.wait_ge(sem("conv_mid"), done)
                j = st.first + st.body * col[0] + c
                w0 = par[:, bass.ds(COL["hy_w"] + j, 1)]
                w2 = par[:, bass.ds(COL["hy_w"] + 48 + j, 1)]
                dve.scalar_tensor_tensor(to[:, 1:T], ps[:, b, 0:T - 1], w0, to[:, 1:T], ALU.mult,
                                         ALU.add).then_inc(sem("conv_left"), 1)
                dve.wait_ge(sem("conv_left"), done)
                return done, w2

            def epilogue(st, i, c):
                oc, col, kind = c // st.per_out, st.body * i + c, st.name
                if (c + 1) % st.per_out:
                    return
                b = oc % st.banks
                got = ps[:, b, 0:st.cols]
                n_used = slab(st, i, c) + 1
                if kind in ("out1", "down1"):
                    dve.wait_ge(slab_used, n_used)
                    j = (st.body // st.per_out) * i + oc
                    dve.tensor_tensor(xT[:, j, 0:T], xT[:, j, 0:T], got, ALU.add)\
                       .then_inc(bank_free[b], 1)
                elif kind[:3] == "hy_" and kind != "hy_out":
                    to = cvt[:, c, :] if kind == "hy_v" else (u if kind == "hy_x1" else x0)[:, col, :]
                    done, w2 = short_taps(c, (i,), st, b, to)
                    dve.scalar_tensor_tensor(to[:, 0:T - 1], ps[:, b, 1:T], w2, to[:, 0:T - 1],
                                             ALU.mult, ALU.add).then_inc(bank_free[b], 1)
                elif kind in ("k2", "q2"):
                    base = 0 if kind == "k2" else 8
                    dve.wait_ge(slab_used, n_used)
                    if kind == "k2":
                        dve.wait_ge(sem("k_ctx_done"), col + 1)
                    part = rot[:, c % 2, 0, :]
                    same = rot[:, c % 2, 1, :]
                    dve.stream_shuffle(part, ps[:, b, 0:T], [(j + 16) % 32 for j in range(32)])\
                       .then_inc(sem("rot_part"), 1)
                    dve.tensor_tensor(same, ps[:, b, 0:T], rope[:, 0, :], ALU.mult)\
                       .then_inc(bank_free[b], 1)
                    dve.wait_ge(sem("rot_part"), base + col + 1)
                    dve.tensor_tensor(part, part, rope[:, 1, :], ALU.mult).then_inc(sem("rot_sin"), 1)
                    dve.wait_ge(sem("rot_sin"), base + col + 1)
                    to = kT if kind == "k2" else qT
                    dve.wait_ge(bank_free[b], uses(st, i, oc) + 1)
                    dve.tensor_tensor(to[:, col, 0:T], same, part, ALU.add).then_inc(sem("rot_done"), 1)
                elif kind == "hy_out":
                    dve.wait_ge(slab_used, n_used)
                    dve.wait_ge(sem("gates_ready"), 1)
                    dve.tensor_tensor(tT[:, col, :], gT[:, col, :], got, ALU.mult)\
                       .then_inc(bank_free[b], 1)
                elif kind == "da_out":
                    dve.wait_ge(slab_used, n_used)
                    dve.wait_ge(sem("gates_ready"), 2)
                    dve.tensor_tensor(tda[:, c, :], gT[:, KD + col, :], got, ALU.mult)\
                       .then_inc(bank_free[b], 1)
                    dve.wait_ge(bank_free[b], uses(st, i, oc) + 1)
                    dve.tensor_tensor(tT[:, col, :], tT[:, col, :], tda[:, c, :], ALU.add)\
                       .then_inc(sem("tT_ready"), 1)

            def stage(name):
                st = stages[name]
                sg, pr, hh, hl = (sg2, pr2, hh2, hl2) if st.cols > T else (sg1, pr1, hh1, hl1)

                def body(i, rides=name in ADA_RIDES):
                    for c in range(st.body):
                        q = c // 2
                        if name[:2] == "up" and c % 2:
                            dve.wait_ge(bank_free[c - 1], uses(st, i, c - 1) + 1)
                            dve.wait_ge(slab_used, slab(st, i, c) + 1)
                            dve.tensor_tensor(pr[:, q, :], sg[:, q, :], ps[:, c, 0:st.cols], ALU.mult)\
                               .then_inc(bank_free[c], 1)
                        nxt = ahead(st, i, c)
                        if nxt:
                            split(*nxt)
                        if name[:2] == "up" and c % 2:
                            dve.wait_ge(sem("hh_done"), pairs_before(name) + 2 * i + q + 1)
                            dve.tensor_tensor(hl[:, 2 * i + q, :], pr[:, q, :],
                                              hh[:, 2 * i + q, :].bitcast(F32), ALU.subtract)\
                               .then_inc(sem("hl_done"), 1)
                        epilogue(st, i, c)
                        if rides and c in (1, 3):
                            modulation(ADA_RIDES[name] + 2 * i + c // 2, c // 2,
                                       ADA_RIDES[name] < N_ADA_BOTH)

                if name in ADA_TRIPS:
                    with dve.Fori(0, ADA_TRIPS[name]) as i:
                        body(i)
                    with dve.Fori(ADA_TRIPS[name], st.trips - 1) as i:
                        body(i, rides=False)
                    body(st.trips - 1, rides=False)
                else:
                    trips(dve, st, body)

            def modulation(n, r, both):
                dve.wait_ge(sem(f"ada_landed{r}"), 8 * (n - r) + 16)
                w = ada[:, r, :].rearrange("p (k n) -> p k n", k=4)

                def total(s, c, waste):
                    return dve.scalar_tensor_tensor(waste, w, 1.0, c, ALU.mult, ALU.mult,
                                                    accum_out=mod[:, bass.ds(n, 1), s])

                if both:
                    total(0, act_c[:, 0:4, T:2 * T], proj[:, 0:4, T:2 * T])\
                        .then_inc(sem("mod_x_summed"), 1)
                    dve.wait_ge(sem("mod_x_summed"), n + 1)
                    total(1, act_c[:, 4:8, T:2 * T], w).then_inc(sem("ada_used"), 1)
                else:
                    total(0, ps[:, 6:8, :].rearrange("p b (k n) -> p (b k) n", k=2), w)\
                        .then_inc(sem("ada_used"), 1)

            def norm(m):
                k0 = NORMS.index(m)
                src, cols, gain, shift = norm_of(m)
                dve.wait_ge(sem("root_ready"), k0 + 1)
                dve.reciprocal(rinv[:, :], rtmp[:, :]).then_inc(sem("rinv_ready"), 1)
                dve.wait_ge(sem("rinv_ready"), k0 + 1)
                if m == "final1":
                    for k in range(KD):
                        dve.scalar_tensor_tensor(xT[:, k, 0:T], xT[:, k, 0:T], gain(k), rinv[:, :],
                                                 ALU.mult, ALU.mult).then_inc(sem("x_updated"), 1)
                    return
                if m in UPDATE:
                    to = slice(T, 2 * T) if m[-1] == "c" else slice(0, T)
                    ks = []

                    def update(k):
                        after(ks[k])
                        dve.tensor_tensor(xT[:, k, to], xT[:, k, to], xg[:, k, :], ALU.add)\
                           .then_inc(sem("x_updated"), 1)

                    for k in range(KD):
                        ks.append(step(dve.scalar_tensor_tensor(
                            xg[:, k, :], proj[:, k, cols], gain(k), rinv[:, :], ALU.mult, ALU.mult)))
                        if k:
                            update(k - 1)
                    update(KD - 1)
                    return
                s = SPLIT.index(m)

                def remainder(k):
                    dve.wait_ge(sem("nh_ready"), 8 * s + k + 1)
                    dve.scalar_tensor_tensor(nl[:, k, cols], xg[:, k, :], shift(k),
                                             nh[:, k, cols].bitcast(F32), ALU.add, ALU.subtract)\
                       .then_inc(sem("nl_ready"), 1)

                for k in range(KD):
                    dve.scalar_tensor_tensor(xg[:, k, :], src[:, k, cols], gain(k), rinv[:, :],
                                             ALU.mult, ALU.mult).then_inc(sem("xg_ready"), 1)
                    if k >= 2:
                        remainder(k - 2)
                remainder(KD - 2)
                remainder(KD - 1)

            dve.memset(small[:, :], 0.0).then_inc(sem("dve_step"), 1)
            n = 1
            two_pi = 2.0 * np.pi
            c1 = float(np.float32(6.28125))
            c2 = float(np.float32(two_pi - c1))
            c3 = float(two_pi - c1 - c2)
            magic = 1.5 * 2.0 ** 23
            dve.wait_ge(sem("par_landed"), 16)
            for l in range(3):
                dve.wait_ge(sem("filt_pre"), l + 1)
                x, t, y = filt[:, 0, :], filt[:, 1, :], filt[:, 2, :]
                k = step(dve.tensor_scalar(x, ps[0:64, 6, 0:T], pc("filt_b", l)[0:64, :],
                                           pc("filt_freq")[0:64, :], ALU.add, ALU.mult))
                after(k)
                k = step(dve.tensor_scalar(t, x, 1.0 / two_pi, magic, ALU.mult, ALU.add))
                after(k)
                k = step(dve.tensor_scalar(t, t, magic, None, ALU.subtract))
                after(k)
                k = step(dve.scalar_tensor_tensor(y, t, -c1, x, ALU.mult, ALU.add))
                after(k)
                k = step(dve.scalar_tensor_tensor(x, t, -c2, y, ALU.mult, ALU.add))
                after(k)
                k = step(dve.scalar_tensor_tensor(y, t, -c3, x, ALU.mult, ALU.add))
                after(k)
                pi = float(np.float32(3.1415925))
                dve.tensor_scalar(filt[:, 3, :], y, pi, -pi, ALU.min, ALU.max).then_inc(sem("sin_arg"), 1)
                if l == 0:
                    dve.wait_ge(sem("c_ready"), 1)
                modulation(l, l % 2, True)
            modulation(3, 1, True)
            split(order[0], 0, 0)
            split(order[0], 0, 1)
            dve.wait_ge(sem("x_landed"), 16)
            dve.wait_ge(sem("par_landed"), 16)
            dve.wait_ge(sem("con_landed"), 16)
            norm("mix1")
            stage("in1_head")
            stage("in1")

            drained(dve, stages["in1"])
            dve.tensor_scalar(dtA[0:6, 2, :], u1[0:6, DT1, :], pc("dt_bias")[0:6, :], None, ALU.add)\
               .then_inc(sem("dt_biased"), 1)
            dve.wait_ge(sem("dt_step"), 3)
            k1 = step(dve.scalar_tensor_tensor(dtA[0:6, 0, :], dtA[0:6, 2, :], 0.0, dtA[0:6, 3, :],
                                               ALU.max, ALU.add))
            after(k1)
            dve.wait_ge(sem("a_ready"), 1)
            dve.tensor_scalar(dtA[0:6, 1, :], dtA[0:6, 0, :], small[0:6, 0:1], -1.0, ALU.mult, ALU.mult)\
               .then_inc(sem("dtA_ready"), 1)
            dve.wait_ge(sem("dtok_ready"), 1)
            k1 = step(dve.tensor_copy(small[:, 160:184], ps[:, STAT, 0:24]))
            after(k1)
            dve.wait_ge(sem("con_landed"), 16)
            for j in range(12):
                ch, h = j // 6, j % 6
                o = 160 + 12 * ch + 6 + h
                dve.tensor_scalar(triA[:, j, :], tri, small[:, o:o + 1], None, ALU.mult)\
                   .then_inc(sem("triA_ready"), 1)

            def conv_tile(j):
                src = u1[:, XBC1 + j, :]
                k = step(dve.tensor_scalar(cT[:, j, :], src, pc("conv_w", 21 + j), pc("conv_b", j),
                                           ALU.mult, ALU.add))
                for lag in (1, 2, 3):
                    after(k)
                    ins = dve.scalar_tensor_tensor(cT[:, j, lag:T], src[:, 0:T - lag],
                                                   pc("conv_w", 7 * (3 - lag) + j), cT[:, j, lag:T],
                                                   ALU.mult, ALU.add)
                    if lag < 3:
                        k = step(ins)
                ins.then_inc(sem("conv1_done"), 1)

            for h in range(HEADS1):
                r = h % 2
                dve.wait_ge(sem("scores_ready"), h + 1)
                if h >= 2:
                    dve.wait_ge(sem("prob_ready"), 2 * h - 2)
                dve.scalar_tensor_tensor(scor[:, r, :], ps[:, r, 0:384], 0.125, cc("mask384", 384),
                                         ALU.mult, ALU.add).then_inc(sem("scores_masked"), 1)
                dve.wait_ge(sem("scores_masked"), h + 1)
                for qt, (a, b) in enumerate(((0, 128), (128, 384))):
                    o = 2 + 2 * h + qt
                    dve.tensor_reduce(small[:, o:o + 1], scor[:, r, a:b], AX.X, ALU.max, negate=True)\
                       .then_inc(sem("nmax_ready"), 1)
                conv_tile(h)
                dve.wait_ge(sem("prob_ready"), 2 * h + 2)
                o = 14 + 2 * h
                k = step(dve.reciprocal(small[:, o + 12:o + 14], small[:, o:o + 2]))
                after(k)
                for qt, (a, b) in enumerate(((0, 128), (128, 384))):
                    dve.tensor_scalar(prob[:, r, a:b], prob[:, r, a:b],
                                      small[:, o + 12 + qt:o + 13 + qt], None, ALU.mult)\
                       .then_inc(sem("prob_scaled"), 1)
            conv_tile(6)
            for m in range(ADA_MIXERS, ADA_RIDES["out1"]):
                modulation(m, m % 2, True)

            def dtok(ch, kind):
                o = 160 + 12 * ch + 6 * kind
                return small[:, o:o + 6]

            dve.wait_ge(sem("xs_ready"), 1)
            for ch in range(2):
                dve.tensor_tensor(xdt[:, ch, :].rearrange("p (h d) -> p h d", h=6),
                                  ps[:, 5 + ch, 0:384].rearrange("p (h d) -> p h d", h=6),
                                  dtok(ch, 0).unsqueeze(2).broadcast_to([P, 6, 64]), ALU.mult)\
                   .then_inc(sem("xdt_ready"), 1)
            dve.wait_ge(sem("acum_ready"), 1)
            k = step(dve.tensor_copy(small[:, 40:64], ps[:, STAT, 32:56]))
            after(k)
            dve.tensor_tensor(small[:, 64:70], small[:, 52:58], small[:, 40:46], ALU.subtract)\
               .then_inc(sem("dte_arg"), 1)
            dve.wait_ge(sem("arow_ready"), 1)
            for j in range(12):
                ch, h = j // 6, j % 6
                if j == 4:
                    dve.wait_ge(sem("ce_exp"), 2)
                dve.scalar_tensor_tensor(seg[:, j, :], ps[:, j // 4, (j % 4) * P:(j % 4) * P + P],
                                         small[:, 40 + 6 * ch + h:41 + 6 * ch + h], cc("maskT", P),
                                         ALU.subtract, ALU.add).then_inc(sem("seg_ready"), 1)
            dve.wait_ge(sem("dte_ready"), 1)
            dve.wait_ge(sem("xdt_ready"), 2)
            dve.tensor_tensor(xw[:, :].rearrange("p (h d) -> p h d", h=6),
                              xdt[:, 0, :].rearrange("p (h d) -> p h d", h=6),
                              small[:, 64:70].unsqueeze(2).broadcast_to([P, 6, 64]), ALU.mult)\
               .then_inc(sem("xw_ready"), 1)
            dve.wait_ge(sem("ce_exp"), 2)
            for g in range(2):
                dve.tensor_tensor(CE[:, 3 * g:3 * g + 3, :], CE[:, 3 * g:3 * g + 3, :],
                                  cT[:, 5 + g, P:2 * P].unsqueeze(1).broadcast_to([P, 3, P]), ALU.mult)\
                   .then_inc(sem("ce_ready"), 1)
            dve.wait_ge(sem("g_ready"), 1)
            dve.wait_ge(sem("decay1_ready"), 1)
            for j in range(4):
                dve.tensor_tensor(seg[:, 3 * j:3 * j + 3, :], seg[:, 3 * j:3 * j + 3, :],
                                  ps[:, 3, j * P:j * P + P].unsqueeze(1).broadcast_to([P, 3, P]), ALU.mult)\
                   .then_inc(sem("m_ready"), 1)
            dve.wait_ge(sem("y1_ready"), 1)
            dve.wait_ge(sem("z_ready"), 1)
            for t in range(3):
                k = step(dve.scalar_tensor_tensor(yssd[:, t, :], cT[:, t, :], pc("d_skip", t),
                                                  ps[:, t, 0:T], ALU.mult, ALU.add))
            after(k)
            dve.tensor_tensor(yssd[:, :, :], yssd[:, :, :], u1[:, Z1:Z1 + 3, :], ALU.mult)\
               .then_inc(sem("gated_ready"), 1)
            dve.wait_ge(sem("yroot_ready"), 1)
            dve.reciprocal(yrg[:, :, :], yroot[:, :, :]).then_inc(sem("yrg_ready"), 1)
            dve.wait_ge(sem("yrg_ready"), 1)
            for t, a, b, g in ((0, 0, 128, 0), (1, 0, 64, 0), (1, 64, 128, 1), (2, 0, 128, 1)):
                ins = dve.scalar_tensor_tensor(mixT[a:b, 3 + t, :], yssd[a:b, t, :],
                                               pc("ssd_norm", t)[a:b, :], yrg[a:b, g, :],
                                               ALU.mult, ALU.mult)
                if t < 2:
                    step(ins)
            ins.then_inc(sem("mix_ready"), 1)
            for m, (a, b) in enumerate(((0, 3), (6, 8), (3, 6))):
                dve.wait_ge(sem("mix_hi"), m + 1)
                dve.tensor_tensor(nl[:, a:b, 0:T], mixT[:, a:b, :], nh[:, a:b, 0:T].bitcast(F32),
                                  ALU.subtract).then_inc(sem("mix_lo"), 1)

            stage("out1")
            norm("ffn1")
            stage("up1")

            dve.tensor_tensor(small[0:64, 80:82], pc("lam_q", 0, 2)[0:64, :], pc("lam_k", 0, 2)[0:64, :],
                              ALU.mult).then_inc(sem("lam_prod"), 1)
            k = step(dve.tensor_scalar(small[:, 84:85], pc("subln"), 1.0 - LAM_INIT, None, ALU.mult))
            after(k)
            stage("down1")
            def gains(rows):
                for row, q, s, g, kind in rows:
                    k = step(dve.scalar_tensor_tensor(
                        gmod[:, row, :], mod[:, 8 * q:8 * q + 8, s], {"scale": 1.0, "half": 0.5, "gate": 1.0}[kind],
                        pc("norm_g", 8 * g, 8), ALU.add if kind == "scale" else ALU.mult, ALU.mult))
                after(k)

            dve.wait_ge(sem("ada_used"), N_ADA_BOTH)
            k = step(dve.tensor_tensor(mod[:, 0:N_ADA_BOTH, :], mod[:, 0:N_ADA_BOTH, :],
                                       pc("b_ada", 0, N_ADA_BOTH).unsqueeze(2).broadcast_to([P, N_ADA_BOTH, 2]),
                                       ALU.add))
            after(k)
            gains([(0, 1, 0, 0, "scale"), (1, 1, 1, 0, "scale"), (2, 2, 0, 1, "half"), (3, 2, 1, 1, "half"),
                   (4, 4, 0, 2, "scale"), (5, 4, 1, 2, "scale")])
            dve.wait_ge(sem("c_moved"), 1)
            norm("pre2c")
            norm("final1")
            norm("pre2x")
            dve.wait_ge(sem("lam_exp"), 1)
            k = step(dve.tensor_tensor(small[:, 85:86], small[:, 83:84], small[:, 82:83], ALU.subtract))
            after(k)
            k = step(dve.tensor_scalar(small[:, 86:87], small[:, 85:86], LAM_INIT, None, ALU.subtract))
            after(k)
            nlam = small[:, 86:87]
            stage("up2")
            stage("down2")
            def filters(g0, g1):
                for g in range(g0, g1):
                    lt, q = g // 4, g % 4
                    dve.wait_ge(sem("h_ready"), g + 1)
                    ins = dve.tensor_tensor(hfb[:, lt, q * 512:q * 512 + 512], ps[:, g % 4, :],
                                            decay[:, lt, (q % 2) * 512:(q % 2) * 512 + 512], ALU.mult)
                    if (lt, q) == (0, 3):
                        after(step(ins))
                        ins = dve.memset(hfb[0:1, 0, D:2 * D], 0.0)
                    ins.then_inc(sem("hfb_ready"), 1)

            norm("post2x")
            dve.wait_ge(sem("decay_landed"), 16)
            filters(0, 4)
            norm("post2c")
            filters(4, 8)
            dve.wait_ge(sem("hfb_ready"), 8)
            for s, op in enumerate((ALU.add, ALU.subtract)):
                dve.tensor_tensor(hsd[:, :, s * D:s * D + D], hfb[:, :, 0:D], hfb[:, :, D:2 * D], op)\
                   .then_inc(sem("hsd_ready"), 1)
            norm("mod2x")
            norm("mod2c")
            dve.wait_ge(sem("rope_landed"), 16)
            stage("k2")
            dve.wait_ge(sem("ksum_ready"), 1)
            after(step(dve.tensor_scalar(small[:, 232:240], ps[:, 5, 256:264], EPS, None, ALU.add)))
            knorm = small[:, 240:248]
            dve.reciprocal(knorm, small[:, 232:240]).then_inc(sem("knorm_ready"), 1)
            for name in ("v2", "q2"):
                stage(name)

            def mix_maps(r):
                a, b = p2[:, r % 2, 0, :], p2[:, r % 2, 1, :]
                dve.wait_ge(sem("prob2_ready"), 2 * r + 2)
                if r:
                    dve.wait_ge(sem("pmix_ready"), r)
                o, inv = 128 + 2 * r, 160 + 2 * r
                k = step(dve.reciprocal(small[:, inv:inv + 2], small[:, o:o + 2]))
                after(k)
                k = step(dve.tensor_scalar(small[:, 226:227], small[:, inv + 1:inv + 2], nlam,
                                           small[:, o:o + 1], ALU.mult, ALU.mult))
                after(k)
                dve.scalar_tensor_tensor(a, b, small[:, 226:227], a, ALU.mult, ALU.add)\
                   .then_inc(sem("pmix_ready"), 1)

            def square_sum(r):
                dve.wait_ge(sem("otok_ready"), r + 1)
                if r >= 1:
                    dve.wait_ge(sem("oss_ready"), r)
                dve.tensor_tensor_reduce(out=rtmp[:, 0:P], in0=otok[:, r, :], in1=otok[:, r, :], scale=1.0,
                                         scalar=0.0, op0=ALU.mult, op1=ALU.add,
                                         accum_out=small[:, 192 + r:193 + r]).then_inc(sem("oss_ready"), 1)

            def largest(r):
                dve.wait_ge(sem("s2_ready"), r + 1)
                o = 228 + 2 * (r % 2)
                after(step(dve.tensor_reduce(small[:, o:o + 2], ps[:, 4:6, :], AX.X, ALU.max)))
                dve.tensor_scalar(small[:, 96 + 2 * r:98 + 2 * r], small[:, o:o + 2], -0.125, None,
                                  ALU.mult).then_inc(sem("nmax2_ready"), 1)

            def spectrum(g):
                ft, half = g // 2, g % 2
                pair = "p (a n) -> p a n"
                w = slice(half * 512, half * 512 + 512)
                kr, ki = kre[:, ft, w].rearrange(pair, a=2), kim[:, ft, w].rearrange(pair, a=2)
                ur, ui = (ps[:, 2 + n, :].rearrange(pair, a=2) for n in range(2))
                t0, t1 = yt[:, 0:2, :], yt[:, 2:4, :]
                dve.wait_ge(sem("uf_ready"), g + 1)
                if g:
                    dve.wait_ge(sem("yf_ready"), g)
                step(dve.tensor_tensor(t0, kr, ur, ALU.mult))
                after(step(dve.tensor_tensor(t1, ki, ui, ALU.mult)))
                after(step(dve.tensor_tensor(halves(proj, ft, half), t0, t1, ALU.subtract)))
                step(dve.tensor_tensor(t0, ki, ur, ALU.mult))
                after(step(dve.tensor_tensor(t1, kr, ui, ALU.mult)))
                dve.tensor_tensor(halves(act_c, ft, half), t0, t1, ALU.add).then_inc(sem("yf_ready"), 1)

            def convolved(j):
                a, b = yt[:, j % 2, :], yt[:, 2 + j % 2, :]
                if j >= 2:
                    dve.wait_ge(sem("yhy_ready"), j - 1)
                step(dve.tensor_scalar(a, u[:, j, :], pc("hy_bias", j), None, ALU.mult))
                dve.wait_ge(sem("yc_ready"), j + 1)
                after(n)
                after(step(dve.scalar_tensor_tensor(b, ps[:, 2 + j % 2, 0:T], knorm[:, j:j + 1], a,
                                                    ALU.mult, ALU.add)))
                dve.tensor_tensor(x0[:, j, :], b, x0[:, j, :], ALU.mult).then_inc(sem("yhy_ready"), 1)

            dve.wait_ge(sem("knorm_ready"), 1)
            for p, st, i, c in woven(stages):
                if p < 32 and p % 2 == 0:
                    largest(p // 2)
                if 21 <= p < 25:
                    spectrum(p - 21)
                if 26 <= p < 34:
                    if p == 26:
                        dve.wait_ge(sem("yf_ready"), 4)
                    convolved(p - 26)
                if 2 <= p <= 32 and p % 2 == 0:
                    epilogue(*late)
                if p < 32 and p % 2 == 0:
                    mix_maps(p // 2)
                split(*ahead(st, i, c))
                if p < 32 and p % 2:
                    late = st, i, c
                else:
                    epilogue(st, i, c)
                if 3 <= p <= 33 and p % 2:
                    square_sum((p - 3) // 2)
                if p == 35:
                    dve.wait_ge(sem("oroot_ready"), 1)
                    after(step(dve.reciprocal(small[:, 144:160], small[:, 208:224])))
                    dve.tensor_tensor(otok[:, :, :], otok[:, :, :],
                                      small[:, 144:160].unsqueeze(2).broadcast_to([P, 2 * HEADS2, P]),
                                      ALU.mult).then_inc(sem("otok_scaled"), 1)
                if p == 36:
                    dve.wait_ge(sem("yhy_hi"), 1)
                    dve.tensor_tensor(nl[:, :, T:2 * T], x0[:, :, :], nh[:, :, T:2 * T].bitcast(F32),
                                      ALU.subtract).then_inc(sem("yhy_lo"), 1)
                if p == 38:
                    dve.wait_ge(sem("ada_used"), N_ADA)
                    k = step(dve.tensor_tensor(mod[:, N_ADA_BOTH:N_ADA, 0], mod[:, N_ADA_BOTH:N_ADA, 0],
                                               pc("b_ada", N_ADA_BOTH, N_ADA - N_ADA_BOTH), ALU.add))
                    after(k)
                    gains([(6, 5, 0, 3, "gate"), (7, 7, 0, 4, "scale"), (8, 8, 0, 5, "half")])
                if p >= 40:
                    j = p - 40
                    dve.wait_ge(sem("o_hi"), j + 1)
                    dve.scalar_tensor_tensor(nl[:, j, 0:T], ps[:, 4 + j % 4, 0:T], small[:, 84:85],
                                             nh[:, j, 0:T].bitcast(F32), ALU.mult, ALU.subtract)\
                       .then_inc(sem("o_lo"), 1)
            st = stages["da_out"]

            def remainder(j):
                dve.wait_ge(sem("t_hi"), j + 1)
                dve.tensor_tensor(nl[:, j, T:2 * T], tT[:, j, :], nh[:, j, T:2 * T].bitcast(F32),
                                  ALU.subtract).then_inc(sem("t_lo"), 1)

            for i in range(2):
                for c in range(4):
                    split(*ahead(st, i, c))
                    epilogue(st, i, c)
                    if 4 * i + c:
                        remainder(4 * i + c - 1)
            remainder(KD - 1)
            stage("o2")
            norm("post_mix2")
            norm("pre3")
            stage("up3")
            stage("down3")
            norm("post3")

        @block.tensor
        def _(pe):
            mm = nc.tensor.matmul

            def dense_token_major(st, i, c):
                h = (st.s0 + c) % HL
                pe.wait_ge(lo_done, slab(st, i, c) + 1)
                for tt in range(4):
                    if c == 0:
                        wait(pe, bank_free[tt], uses(st, i, tt))
                    tk = slice(tt * P, tt * P + P)
                    for k in range(2):
                        wk, kk = slice(k * 512, k * 512 + 512), 2 * c + k
                        mm(ps[:, tt, :], nh[:, kk, tk], hi[:, h, wk], start=kk == 0, stop=False)
                        mm(ps[:, tt, :], nh[:, kk, tk], lo[:, h, wk], start=False, stop=False)
                        m = mm(ps[:, tt, :], nl[:, kk, tk], hi[:, h, wk], start=False,
                               stop=kk == KD - 1)
                m.then_inc(slab_used, 1)

            def dense(st, i, c, x_hi, x_lo, ready=None):
                s, h = slab(st, i, c), (st.s0 + c) % HL
                oc, part = c // st.per_out, c % st.per_out
                b = oc % st.banks
                pe.wait_ge(lo_done, s + 1)
                if part == 0:
                    wait(pe, bank_free[b], uses(st, i, oc))
                for k in range(st.kt):
                    wk = slice(k * P, k * P + P)
                    kk = part * st.kt + k
                    first = part == 0 and k == 0
                    last = part == st.per_out - 1 and k == st.kt - 1
                    o = ps[:, b, 0:st.cols]
                    if ready:
                        ready(kk)
                    mm(o, hi[:, h, wk], x_hi[:, kk, 0:st.cols], start=first, stop=False)
                    mm(o, lo[:, h, wk], x_hi[:, kk, 0:st.cols], start=False, stop=False)
                    m = mm(o, hi[:, h, wk], x_lo[:, kk, 0:st.cols], start=False, stop=last)
                m.then_inc(slab_used, 1)

            def stage(name, x_hi=nh, x_lo=nl, ready=None):
                st = stages[name]

                def body(i, ready=None):
                    for c in range(st.body):
                        if name == "v2":
                            dense_token_major(st, i, c)
                        else:
                            dense(st, i, c, x_hi, x_lo, ready if c < st.per_out else None)

                first = 0
                if ready or st.trips == 1:
                    body(0, ready)
                    first = 1
                if first < st.trips:
                    with pe.Fori(first, st.trips) as i:
                        body(i)

            def norm(m):
                n = NORMS.index(m)
                wait(pe, sem("root_ready"), n)
                for k in range(KD):
                    pe.wait_ge(sem("sq_ready"), 8 * n + k + 1)
                    o = mm(ps[:, STAT, 0:T], ones, sq[:, k, :], start=(k == 0), stop=(k == KD - 1))
                o.then_inc(sem("stat_ready"), 1)

            def normed(m):
                return lambda k: pe.wait_ge(sem("nl_ready"), 8 * SPLIT.index(m) + k + 1)

            pe.wait_ge(sem("z_landed"), 16)
            pe.wait_ge(sem("par_landed"), 16)
            for l in range(3):
                w = pc(f"filt_w{l + 1}", 0, 64)
                wait(pe, sem("sin_ready"), l)
                mm(ps[0:64, 6, 0:T], w[0:33, :] if l == 0 else w[0:64, :],
                   zT[0:33, :] if l == 0 else filt3[:, :], start=True, stop=True)\
                    .then_inc(sem("filt_pre"), 1)
            pe.wait_ge(sem("con_landed"), 16)
            norm("mix1")
            stage("in1_head", ready=normed("mix1"))
            stage("in1")

            drained(pe, stages["in1"])
            for tt in range(2):
                for j in range(NT1):
                    o = pe.transpose(ps[:, 5 + tt, j * P:j * P + P],
                                     u1[:, V1 + j, tt * P:tt * P + P], ident)
            o.then_inc(sem("vt_ready"), 1)

            def scores(h):
                t, a = h // 2, 64 * (h % 2)
                q, k = u1[a:a + 64, Q1 + t, :], u1[a:a + 64, K1 + t, :]
                if h >= 2:
                    pe.wait_ge(sem("scores_masked"), h - 1)
                mm(ps[:, h % 2, 0:P], q[:, 0:P], k[:, 0:P], start=True, stop=True)
                mm(ps[:, h % 2, P:3 * P], q[:, P:T], k[:, 0:T], start=True, stop=True)\
                    .then_inc(sem("scores_ready"), 1)

            def turn_probs(h):
                pe.wait_ge(sem("prob_scaled"), 2 * h + 2)
                if h >= 2:
                    pe.wait_ge(sem("pt_copied"), h - 1)
                for j in range(3):
                    o = pe.transpose(ps[:, 2 + h % 2, j * P:j * P + P],
                                     prob[:, h % 2, j * P:j * P + P], ident)
                o.then_inc(sem("pt_ready"), 1)

            def values(h):
                t, a = h // 2, 64 * (h % 2)
                pe.wait_ge(sem("pt_copied"), h + 1)
                if h == 0:
                    pe.wait_ge(sem("vtok_copied"), 1)
                if h == 4:
                    pe.wait_ge(sem("o1_copied"), 1)
                mm(ps[a:a + 64, 5 + t % 2, 0:T], vtok[:, 0, 64 * h:64 * h + 64], pT[:, h % 2, 0:T],
                   start=True, stop=False)
                mm(ps[a:a + 64, 5 + t % 2, P:T], vtok[:, 1, 64 * h:64 * h + 64], pT[:, h % 2, T:3 * P],
                   start=False, stop=True).then_inc(sem("o1_ready"), 1)

            scores(0)
            pe.wait_ge(sem("dtA_ready"), 1)
            for ch in range(2):
                for kind in range(2):
                    o = pe.transpose(ps[:, STAT, 12 * ch + 6 * kind:12 * ch + 6 * kind + 6],
                                     dtA[0:6, kind, ch * P:ch * P + P], ident[0:6, 0:6])
            o.then_inc(sem("dtok_ready"), 1)
            for h in range(HEADS1):
                if h + 1 < HEADS1:
                    scores(h + 1)
                turn_probs(h)
                if h >= 1:
                    values(h - 1)
            values(HEADS1 - 1)

            pe.wait_ge(sem("triA_ready"), 12)
            for ch in range(2):
                mm(ps[:, STAT, 32 + 6 * ch:38 + 6 * ch], tri, small[:, 166 + 12 * ch:172 + 12 * ch],
                   start=True, stop=True)
            for ch in range(2):
                o = mm(ps[:, STAT, 44 + 6 * ch:50 + 6 * ch], ones, small[:, 166 + 12 * ch:172 + 12 * ch],
                       start=True, stop=True)
            o.then_inc(sem("acum_ready"), 1)
            pe.wait_ge(sem("pt_copied"), HEADS1)
            pe.wait_ge(sem("scores_masked"), HEADS1)
            for b in range(3):
                o = mm(ps[:, b, :], ones, triA[:, 4 * b:4 * b + 4, :].rearrange("p a n -> p (a n)"),
                       start=True, stop=True)
            o.then_inc(sem("arow_ready"), 1)
            pe.wait_ge(sem("cT_ready"), 1)
            pe.wait_ge(sem("o1_copied"), 3)
            for tt in range(2):
                for j in range(NT1):
                    o = pe.transpose(ps[:, 5 + tt, j * P:j * P + P], cT[:, j, tt * P:tt * P + P], ident)
            o.then_inc(sem("xs_ready"), 1)
            pe.wait_ge(sem("dte_arg"), 1)
            for g in range(2):
                o = pe.transpose(ps[:, STAT, 64 + g * P:64 + g * P + P], cT[:, 3 + g, 0:P], ident)
            o.then_inc(sem("bt_ready"), 1)
            for ch in range(2):
                for g in range(2):
                    w = slice(ch * P, ch * P + P)
                    o = mm(ps[:, 3, (2 * ch + g) * P:(2 * ch + g) * P + P], cT[:, 3 + g, w],
                           cT[:, 5 + g, w], start=True, stop=True)
            o.then_inc(sem("g_ready"), 1)
            pe.wait_ge(sem("pool_in_ready"), 4)
            pe.wait_ge(sem("poolw_landed"), 16)
            pe.wait_ge(sem("xdt_ready"), 2)
            for t in range(2):
                o = mm(ps[:, 6, t * T:t * T + T], poolw[:, t, :], pools[:, t, :], start=True, stop=True)
            o.then_inc(sem("pool_ready"), 1)
            pe.wait_ge(sem("btok_copied"), 1)
            pe.wait_ge(sem("xw_ready"), 1)
            for g in range(2):
                o = mm(ps[:, 5, 192 * g:192 * g + 192], btok[:, g, :], xw[:, 192 * g:192 * g + 192],
                       start=True, stop=True)
            o.then_inc(sem("prev_ready"), 1)
            pe.wait_ge(sem("prev_copied"), 1)
            pe.wait_ge(sem("m_ready"), 4)
            pe.wait_ge(sem("ce_ready"), 2)
            for h in range(HEADS1):
                t, a = h // 2, 64 * (h % 2)
                w = slice(64 * h, 64 * h + 64)
                mm(ps[a:a + 64, t, 0:P], xdt[:, 0, w], seg[:, h, :], start=True, stop=True)
                mm(ps[a:a + 64, t, P:T], xdt[:, 1, w], seg[:, 6 + h, :], start=True, stop=False)
                o = mm(ps[a:a + 64, t, P:T], prev[:, w], CE[:, h, :], start=False, stop=True)
            o.then_inc(sem("y1_ready"), 1)
            pe.wait_ge(sem("ysq_ready"), 1)
            mm(ps[:, 3, 0:T], ones, ysq[:, 0, :], start=True, stop=False)
            mm(ps[:, 3, 0:T], ones[0:64, :], ysq[0:64, 1, :], start=False, stop=True)
            mm(ps[:, STAT, 0:T], ones, ysq[:, 2, :], start=True, stop=False)
            mm(ps[:, STAT, 0:T], ones[64:128, :], ysq[64:128, 1, :], start=False, stop=True)\
                .then_inc(sem("ystat_ready"), 1)

            pe.wait_ge(sem("mix_lo"), 3)
            stage("out1")
            pe.wait_ge(sem("yroot_ready"), 1)
            norm("ffn1")
            stage("up1", ready=normed("ffn1"))
            pe.wait_ge(sem("hl_done"), KH)
            stage("down1", hh1, hl1)
            pe.wait_ge(sem("lam_prod"), 1)
            mm(ps[:, 5, 0:2], ones[0:64, :], small[0:64, 80:82], start=True, stop=True)\
                .then_inc(sem("lam_dots"), 1)
            norm("pre2c")
            norm("final1")
            norm("pre2x")
            stage("up2", ready=normed("pre2x"))
            pe.wait_ge(sem("hl_done"), 2 * KH)
            stage("down2", hh2, hl2)
            def filters(g0, g1):
                for g in range(g0, g1):
                    lt, q = g // 4, g % 4
                    wait(pe, sem("hfb_ready"), g - 3)
                    mm(ps[:, g % 4, :], filt3[:, lt * P:lt * P + P], w4[:, q * 512:q * 512 + 512],
                       start=True, stop=True).then_inc(sem("h_ready"), 1)

            norm("post2x")
            drained(pe, stages["down2"])
            pe.wait_ge(sem("w4_landed"), 16)
            filters(0, 4)
            norm("post2c")
            filters(4, 8)
            norm("mod2x")
            pe.wait_ge(sem("dft_landed"), 16)
            pe.wait_ge(sem("hsd_ready"), 2)
            for g in range(8):
                kind, ft, half = g // 4, g % 4 // 2, g % 2
                if g == 4:
                    norm("mod2c")
                wait(pe, sem("kf_copied"), g - 3)
                for tt in range(2):
                    o = mm(ps[:, g % 4, :], dft[:, 2 * kind + tt, ft * P:ft * P + P],
                           hsd[:, tt, D * kind + half * 512:D * kind + half * 512 + 512],
                           start=(tt == 0), stop=(tt == 1))
                o.then_inc(sem("kf_ready"), 1)
            pe.wait_ge(sem("kf_copied"), 8)
            stage("k2", ready=normed("mod2c"))
            pe.wait_ge(sem("abs_summed"), 1)
            for j in range(KD):
                o = mm(ps[:, 5, 256 + j:257 + j], absk[:, 0, j * P:j * P + P], ones[:, 0:1],
                       start=True, stop=True)
            o.then_inc(sem("ksum_ready"), 1)
            stage("v2")
            stage("q2")
            pe.wait_ge(sem("rot_done"), 16)

            def scores2(r):
                h, qt = r // 2, r % 2
                wait(pe, sem("prob2_ready"), 2 * r)
                for m in range(2):
                    a = 64 * m
                    o = mm(ps[:, 4 + m, :], qT[a:a + 64, h, qt * P:qt * P + P],
                           kT[a:a + 64, h, :], start=True, stop=True)
                o.then_inc(sem("s2_ready"), 1)

            def turn2(r):
                pe.wait_ge(sem("pmix_ready"), r + 1)
                wait(pe, sem("pt2_copied"), r)
                for kt in range(4):
                    o = pe.transpose(ps[:, 6, kt * P:kt * P + P],
                                     p2[:, r % 2, 0, kt * P:kt * P + P], ident)
                o.then_inc(sem("pt2_ready"), 1)

            def values2(r):
                h = r // 2
                pe.wait_ge(sem("pt2_copied"), r + 1)
                wait(pe, sem("otok_ready"), r)
                for kt in range(4):
                    o = mm(ps[:, 7, 0:P], pT2[:, r % 2, kt, :], V[:, kt, h * P:h * P + P],
                           start=(kt == 0), stop=(kt == 3))
                o.then_inc(sem("o2_ready"), 1)

            def turn_u(g):
                tt, half = g // 2, g % 2
                pe.wait_ge(sem("u_ready"), KD)
                wait(pe, sem("ut_copied"), g - 1)
                for j in range(4):
                    o = pe.transpose(ps[:, 2 + g % 2, j * P:j * P + P],
                                     u[:, 4 * half + j, tt * P:tt * P + P], ident)
                o.then_inc(sem("ut_ready"), 1)

            def spectrum(g):
                ft, half = g // 2, g % 2
                pe.wait_ge(sem("ut_copied"), 4)
                wait(pe, sem("yf_ready"), g)
                for kind in range(2):
                    for tt in range(2):
                        o = mm(ps[:, 2 + kind, :], dft[:, 2 * kind + tt, ft * P:ft * P + P],
                               halves(xT, tt, half), start=(tt == 0), stop=(tt == 1))
                o.then_inc(sem("uf_ready"), 1)

            def inverse(j):
                pe.wait_ge(sem("yf_ready"), 4)
                wait(pe, sem("yhy_ready"), j - 1)
                for n in range(4):
                    y = proj if n < 2 else act_c
                    r, w = 4 * (n % 2) + j // 2, T + P * (j % 2)
                    o = mm(ps[:, 2 + j % 2, 0:T], y[:, r, w:w + P], dft[:, 4 + n, :],
                           start=(n == 0), stop=(n == 3))
                o.then_inc(sem("yc_ready"), 1)

            for p, st, i, c in woven(stages):
                if p < 32 and p % 2 == 0:
                    scores2(p // 2)
                if p < 40:
                    dense(st, i, c, nh, nl)
                else:
                    if p == 40:
                        pe.wait_ge(sem("yhy_lo"), 1)
                    dense(st, i, c, nh[:, :, T:2 * T], nl[:, :, T:2 * T])
                if 2 <= p <= 32 and p % 2 == 0:
                    values2(p // 2 - 1)
                elif p < 32 and p % 2:
                    turn2(p // 2)
                if 16 <= p < 20:
                    turn_u(p - 16)
                if 20 <= p < 24:
                    spectrum(p - 20)
                if 25 <= p < 33:
                    inverse(p - 25)
                if p >= 40:
                    j = p - 40
                    pe.wait_ge(sem("otok_scaled"), 1)
                    wait(pe, sem("o_lo"), j - 3)
                    for qt in range(2):
                        o = pe.transpose(ps[:, 4 + j % 4, qt * P:qt * P + P], otok[:, 2 * j + qt, :], ident)
                    o.then_inc(sem("ott_ready"), 1)
            pe.wait_ge(sem("o_lo"), KD)
            stage("da_out")
            pe.wait_ge(sem("t_lo"), KD)
            stage("o2", nh[:, :, T:2 * T], nl[:, :, T:2 * T])
            norm("post_mix2")
            norm("pre3")
            stage("up3", ready=normed("pre3"))
            pe.wait_ge(sem("hl_done"), 3 * KH)
            stage("down3", hh1, hl1)
            norm("post3")


def pairs_before(name):
    return {"up1": 0, "up2": KH, "up3": 2 * KH}[name]


def slabs_of(w):
    k, n = w.shape
    return np.ascontiguousarray(w.reshape(k // P, P, n // P, P).transpose(2, 1, 0, 3)
                                .reshape(n // P, P, k))


def pair_slabs(w):
    s = slabs_of(w)
    n = s.shape[0] // 2
    return np.ascontiguousarray(np.stack([s[:n], s[n:]], axis=1).reshape(s.shape))


def half_slabs(w):
    s = slabs_of(w)
    return np.ascontiguousarray(s.reshape(KD, P, 2, KHH * P).transpose(0, 2, 1, 3)
                                .reshape(2 * KD, P, KHH * P))


def tiles(v):
    return v.reshape(-1, P).T


def kernel(**inputs):
    import concourse.bacc as bacc
    from concourse.bass_utils import run_bass_kernel_spmd

    g = {k: np.asarray(v) for k, v in inputs.items()}
    w_in = g["w_in"][0]
    n_dt = 6
    qkvzx, dt, pool = w_in[:, :2432], w_in[:, 2432:2438], w_in[:, 2438:]
    dt_pad = np.zeros((D, P), np.float32)
    dt_pad[:, :n_dt] = dt
    in1 = slabs_of(np.concatenate([qkvzx[:, 2048:], pool, dt_pad, qkvzx[:, :2048]], axis=1))

    params = np.zeros((P, NPAR), np.float32)

    def put(name, a, k=0):
        params[:a.shape[0], COL[name] + k:COL[name] + k + a.shape[1]] = a

    for name in ("norm_mix", "norm_ffn", "conv_w", "conv_b", "ssd_norm", "pool_scale"):
        put(name, tiles(g[name][0]))
    put("norm_final", tiles(g["norm_final"]))
    put("d_skip", tiles(np.repeat(g["d_skip"][0], 64)))
    put("b_ada", tiles(g["b_ada_2"][0]))
    put("norm_g", tiles(g["norm_g_2"][0]))
    put("hy_w", tiles(g["hy_conv_w_2"][0]))
    put("hy_b", tiles(g["hy_conv_b_2"][0]))
    put("hy_bias", tiles(g["hy_bias_2"][0]))
    for l in range(3):
        put("filt_b", g[f"filt_b{l + 1}_2"][0][:, None], l)
        put(f"filt_w{l + 1}", g[f"filt_w{l + 1}_2"][0])
    put("filt_freq", g["filt_freq_2"][0][:, None])
    put("subln", g["subln_g_2"][0][:, None])
    put("dt_bias", g["dt_bias"][0][:, None])
    put("a_log", g["a_log"][0][:, None])
    for n in (1, 2):
        put("lam_q", g[f"lambda_q{n}_2"][0][:, None], n - 1)
        put("lam_k", g[f"lambda_k{n}_2"][0][:, None], n - 1)
    pool_w = np.zeros((P, 2, P), np.float32)
    for n in range(4):
        a = 64 * (n % 2)
        pool_w[a:a + 64, n // 2, a:a + 64] = g["pool_w"][0, n]

    def tokens(a):
        return np.ascontiguousarray(a.T.reshape(KD, P, T).transpose(1, 0, 2))

    w_in2 = slabs_of(g["w_in_2"][0])
    v0 = P * IN2["v2"]
    w_in2[IN2["v2"]:IN2["v2"] + 8] = (g["w_in_2"][0][:, v0:v0 + D].reshape(4, 2, P, 2, 512)
                                      .transpose(3, 0, 2, 1, 4).reshape(8, P, D))
    arrays = dict(
        x=tokens(g["x"][0]), ctx=tokens(g["ctx_2"][0]), params=params, pool_w=pool_w,
        cvec=np.tile(np.stack([g["c_2"][0], g["c_ctx_2"]]).reshape(1, KD, T), (P, 1, 1)),
        in1=in1, out1=slabs_of(g["w_out"][0]), up1=pair_slabs(g["w_gate_up"][0]),
        down1=half_slabs(g["w_down"][0]), 
        w_ada=np.ascontiguousarray(g["w_ada_2"][0].T).reshape(72, P, D),
        up2=pair_slabs(g["w_ff_in_2"][0, 0]), down2=half_slabs(g["w_ff_out_2"][0, 0]),
        up3=pair_slabs(g["w_ff_in_2"][0, 1]), down3=half_slabs(g["w_ff_out_2"][0, 1]),
        in2=w_in2, hy_out=slabs_of(g["w_hy_out_2"][0]), da_out=slabs_of(g["w_da_out_2"][0]),
        o2=slabs_of(g["w_o_2"][0]), filt_w4=g["filt_w4_2"][0], **constants())

    nc = bacc.Bacc("TRN2", target_bir_lowering=False, num_devices=1)
    d = {n: nc.dram_tensor(f"in_{n}", a.shape, F32, kind="ExternalInput").ap() for n, a in arrays.items()}
    out = nc.dram_tensor("out_xT", (P, KD, T), F32, kind="ExternalOutput").ap()
    build(nc, d, out)
    r = run_bass_kernel_spmd(nc, [{f"in_{n}": a for n, a in arrays.items()}], core_ids=[0])
    y = r.results[0]["out_xT"]
    return y.transpose(2, 1, 0).reshape(1, T, D)
```
